# Optimizing a Trainium2 kernel written in Bass

```python
import math
import jax, jax.numpy as jnp
from jax import lax
import numpy as np

D_MODEL = 1024
BATCH = 1
SEQ = 256
DEPTH = 1

HEAD_DIM = 64
SWA_Q_HEADS = 8
SWA_KV_HEADS = 2
SWA_GROUP = SWA_Q_HEADS // SWA_KV_HEADS
WINDOW = 128
FOX_HEADS = 4
MLA_HEADS = 4
MLA_Q_RANK = 256
MLA_KV_RANK = 128
MLA_NOPE_DIM = 64
MLA_ROPE_DIM = 32
MLA_V_DIM = 64
ROPE_THETA = 10000.0
REL_BUCKETS = 32
REL_MAX_DIST = 128
D_FF = 2816
CONV_WIDTH = 3
Q_BLOCK = 128
EPS = 1e-6
NEG_INF = -1e30

SWA_WIDTH = SWA_Q_HEADS * HEAD_DIM
FOX_WIDTH = FOX_HEADS * HEAD_DIM
MLA_WIDTH = MLA_HEADS * MLA_V_DIM
MIX_WIDTH = SWA_WIDTH + FOX_WIDTH + MLA_WIDTH
SWA_COLS = (SWA_Q_HEADS + 2 * SWA_KV_HEADS) * HEAD_DIM
FOX_COLS = 3 * FOX_HEADS * HEAD_DIM + FOX_HEADS
MLA_COLS = MLA_Q_RANK + MLA_KV_RANK + MLA_ROPE_DIM
IN_COLS = SWA_COLS + FOX_COLS + MLA_COLS
MLA_QK_DIM = MLA_NOPE_DIM + MLA_ROPE_DIM


def rmsnorm(x, g):
    xf = x.astype(jnp.float32)
    y = xf * lax.rsqrt(jnp.mean(xf * xf, axis=-1, keepdims=True) + EPS) * g.astype(jnp.float32)
    return y.astype(x.dtype)

def t5_causal_bucket(dist):
    max_exact = REL_BUCKETS // 2
    d = jnp.maximum(dist, 0)
    log_ratio = jnp.log(jnp.maximum(d, 1).astype(jnp.float32) / max_exact) / math.log(REL_MAX_DIST / max_exact)
    large = max_exact + (log_ratio * (REL_BUCKETS - max_exact)).astype(jnp.int32)
    large = jnp.minimum(large, REL_BUCKETS - 1)
    return jnp.where(d < max_exact, d, large)

def apply_rope(t, cos, sin):
    t1, t2 = jnp.split(t, 2, axis=-1)
    return jnp.concatenate([t1 * cos - t2 * sin, t1 * sin + t2 * cos], axis=-1)

def swa_sink_attention(q, k, v, sinks, rel_bias):
    B, S = q.shape[0], q.shape[1]
    nb = S // WINDOW
    qb = q.reshape(B, nb, WINDOW, SWA_KV_HEADS, SWA_GROUP, HEAD_DIM)

    def band(t):
        tb = t.reshape(B, nb, WINDOW, SWA_KV_HEADS, HEAD_DIM)
        prev = jnp.pad(tb, ((0, 0), (1, 0), (0, 0), (0, 0), (0, 0)))[:, :-1]
        return jnp.concatenate([prev, tb], axis=2)

    kb, vb = band(k), band(v)
    qi = jnp.arange(WINDOW, dtype=jnp.int32)[:, None] + WINDOW
    kj = jnp.arange(2 * WINDOW, dtype=jnp.int32)[None, :]
    dist = qi - kj
    in_band = (dist >= 0) & (dist < WINDOW)
    valid_key = (jnp.arange(nb)[:, None, None] > 0) | (kj >= WINDOW)[None]
    mask = in_band[None] & valid_key
    bias = rel_bias.astype(jnp.float32)[t5_causal_bucket(dist)]
    bias = bias.transpose(2, 0, 1).reshape(SWA_KV_HEADS, SWA_GROUP, WINDOW, 2 * WINDOW)
    s = jnp.einsum('bnqhgd,bnkhd->bnhgqk', qb, kb, preferred_element_type=jnp.float32)
    s = s * (HEAD_DIM ** -0.5) + bias
    s = jnp.where(mask[None, :, None, None], s, NEG_INF)
    sink = sinks.astype(jnp.float32).reshape(1, 1, SWA_KV_HEADS, SWA_GROUP, 1, 1)
    sink = jnp.broadcast_to(sink, s.shape[:-1] + (1,))
    p = jax.nn.softmax(jnp.concatenate([s, sink], axis=-1), axis=-1)[..., :-1]
    o = jnp.einsum('bnhgqk,bnkhd->bnqhgd', p.astype(v.dtype), vb)
    return o.reshape(B, S, SWA_Q_HEADS * HEAD_DIM)

def blocked_causal_attention(q, k, v, scale, log_forget_cum=None):
    B, S, H = q.shape[0], q.shape[1], q.shape[2]
    nb = S // Q_BLOCK
    q_blocks = q.reshape(B, nb, Q_BLOCK, H, q.shape[-1]).swapaxes(0, 1)
    k_pos = jnp.arange(S, dtype=jnp.int32)
    if log_forget_cum is None:
        f_blocks, f_keys = None, None
    else:
        f_t = log_forget_cum.transpose(0, 2, 1)
        f_blocks = f_t.reshape(B, H, nb, Q_BLOCK).transpose(2, 0, 1, 3)
        f_keys = f_t

    def one_block(args):
        qb, fb, i = args
        s = jnp.einsum('bqhd,bkhd->bhqk', qb, k, preferred_element_type=jnp.float32) * scale
        if fb is not None:
            s = s + (fb[..., :, None] - f_keys[..., None, :])
        q_pos = i * Q_BLOCK + jnp.arange(Q_BLOCK, dtype=jnp.int32)
        s = jnp.where(k_pos[None, :] <= q_pos[:, None], s, NEG_INF)
        p = jax.nn.softmax(s, axis=-1)
        return jnp.einsum('bhqk,bkhd->bqhd', p.astype(v.dtype), v)

    out = lax.map(one_block, (q_blocks, f_blocks, jnp.arange(nb, dtype=jnp.int32)))
    return out.swapaxes(0, 1).reshape(B, S, H * v.shape[-1])

def causal_depthwise_conv(u, w, b):
    S = u.shape[1]
    up = jnp.pad(u, ((0, 0), (CONV_WIDTH - 1, 0), (0, 0)))
    y = b.astype(u.dtype)
    for tap in range(CONV_WIDTH):
        y = y + w[tap].astype(u.dtype) * up[:, tap:tap + S]
    return y

def first_inputs(seed: int = 0) -> dict:
    key = jax.random.key(seed)
    ks = jax.random.split(key, 20)
    L, D = DEPTH, D_MODEL
    f32 = jnp.float32

    def nrm(k, shape, scale):
        return jax.random.normal(k, shape, f32) * scale

    def gain(k, shape):
        return 1.0 + 0.05 * jax.random.normal(k, shape, f32)

    return {
        "x": jax.random.normal(ks[0], (BATCH, SEQ, D), f32),
        "attn_pre_norm": gain(ks[1], (L, D)),
        "w_in": nrm(ks[2], (L, D, IN_COLS), D ** -0.5),
        "forget_bias": 2.0 + 0.5 * jax.random.normal(ks[3], (L, FOX_HEADS), f32),
        "swa_sinks": nrm(ks[4], (L, SWA_Q_HEADS), 0.5),
        "rel_bias": nrm(ks[5], (REL_BUCKETS, SWA_Q_HEADS), 0.5),
        "q_latent_norm": gain(ks[6], (L, MLA_Q_RANK)),
        "w_uq": nrm(ks[7], (L, MLA_Q_RANK, MLA_HEADS * MLA_QK_DIM), MLA_Q_RANK ** -0.5),
        "kv_latent_norm": gain(ks[8], (L, MLA_KV_RANK)),
        "w_ukv": nrm(ks[9], (L, MLA_KV_RANK, MLA_HEADS * (MLA_NOPE_DIM + MLA_V_DIM)), MLA_KV_RANK ** -0.5),
        "group_norm": gain(ks[10], (L, MIX_WIDTH)),
        "w_out": nrm(ks[11], (L, MIX_WIDTH, D), MIX_WIDTH ** -0.5),
        "attn_post_norm": gain(ks[12], (L, D)),
        "ffn_pre_norm": gain(ks[13], (L, D)),
        "w_up": nrm(ks[14], (L, D, 2 * D_FF), D ** -0.5),
        "conv_w": nrm(ks[15], (L, CONV_WIDTH, 2 * D_FF), CONV_WIDTH ** -0.5),
        "conv_b": nrm(ks[16], (L, 2 * D_FF), 0.02),
        "w_down": nrm(ks[17], (L, D_FF, D), D_FF ** -0.5),
        "ffn_post_norm": gain(ks[18], (L, D)),
    }

def first_block(x, attn_pre_norm, w_in, forget_bias, swa_sinks, rel_bias, q_latent_norm, w_uq,
              kv_latent_norm, w_ukv, group_norm, w_out, attn_post_norm, ffn_pre_norm, w_up,
              conv_w, conv_b, w_down, ffn_post_norm):
    B, S, _ = x.shape
    pos = jnp.arange(S, dtype=jnp.float32)
    inv_freq = ROPE_THETA ** (-(jnp.arange(MLA_ROPE_DIM // 2, dtype=jnp.float32) * 2.0 / MLA_ROPE_DIM))
    ang = pos[:, None] * inv_freq[None, :]
    cos = jnp.cos(ang)[:, None, :].astype(x.dtype)
    sin = jnp.sin(ang)[:, None, :].astype(x.dtype)

    for l in range(DEPTH):
        h = rmsnorm(x, attn_pre_norm[l])
        proj = h @ w_in[l]
        a_cols, f_cols, m_cols = jnp.split(proj, [SWA_COLS, SWA_COLS + FOX_COLS], axis=-1)

        qa, ka, va = jnp.split(a_cols, [SWA_WIDTH, SWA_WIDTH + SWA_KV_HEADS * HEAD_DIM], axis=-1)
        out_a = swa_sink_attention(qa.reshape(B, S, SWA_Q_HEADS, HEAD_DIM),
                                   ka.reshape(B, S, SWA_KV_HEADS, HEAD_DIM),
                                   va.reshape(B, S, SWA_KV_HEADS, HEAD_DIM),
                                   swa_sinks[l], rel_bias)

        qf, kf, vf, f_logit = jnp.split(f_cols, [FOX_WIDTH, 2 * FOX_WIDTH, 3 * FOX_WIDTH], axis=-1)
        log_f = jax.nn.log_sigmoid(f_logit.astype(jnp.float32) + forget_bias[l].astype(jnp.float32))
        F = jnp.cumsum(log_f, axis=1)
        out_b = blocked_causal_attention(qf.reshape(B, S, FOX_HEADS, HEAD_DIM),
                                         kf.reshape(B, S, FOX_HEADS, HEAD_DIM),
                                         vf.reshape(B, S, FOX_HEADS, HEAD_DIM),
                                         HEAD_DIM ** -0.5, log_forget_cum=F)

        c_q, c_kv, k_rope = jnp.split(m_cols, [MLA_Q_RANK, MLA_Q_RANK + MLA_KV_RANK], axis=-1)
        qm = (rmsnorm(c_q, q_latent_norm[l]) @ w_uq[l]).reshape(B, S, MLA_HEADS, MLA_QK_DIM)
        q_nope, q_rope = jnp.split(qm, [MLA_NOPE_DIM], axis=-1)
        kv = (rmsnorm(c_kv, kv_latent_norm[l]) @ w_ukv[l]).reshape(B, S, MLA_HEADS, MLA_NOPE_DIM + MLA_V_DIM)
        k_nope, vm = jnp.split(kv, [MLA_NOPE_DIM], axis=-1)
        q_rope = apply_rope(q_rope, cos, sin)
        k_rope = jnp.broadcast_to(apply_rope(k_rope[:, :, None, :], cos, sin), (B, S, MLA_HEADS, MLA_ROPE_DIM))
        out_c = blocked_causal_attention(jnp.concatenate([q_nope, q_rope], axis=-1),
                                         jnp.concatenate([k_nope, k_rope], axis=-1),
                                         vm, MLA_QK_DIM ** -0.5)

        g_a, g_b, g_c = jnp.split(group_norm[l], [SWA_WIDTH, SWA_WIDTH + FOX_WIDTH])
        mixed = jnp.concatenate([rmsnorm(out_a, g_a), rmsnorm(out_b, g_b), rmsnorm(out_c, g_c)], axis=-1)
        x = x + rmsnorm(mixed @ w_out[l], attn_post_norm[l])

        h = rmsnorm(x, ffn_pre_norm[l])
        u = causal_depthwise_conv(h @ w_up[l], conv_w[l], conv_b[l])
        gate, up = jnp.split(u, 2, axis=-1)
        y = (jax.nn.gelu(gate, approximate=True) * up) @ w_down[l]
        x = x + rmsnorm(y, ffn_post_norm[l])
    return x


GLA_HEADS = 4
GLA_DK = 64
GLA_DV = 128
GLA_KEY_W = GLA_HEADS * GLA_DK
GLA_VAL_W = GLA_HEADS * GLA_DV
GLA_GATE_RANK = 16
GLA_GATE_NORMALIZER = 16.0
GLA_CHUNK = 64
POOL_GROUPS = 4
POOL_WINDOWS = (2, 4, 8, 16)
POOL_W = D_MODEL // 2
POOL_GW = POOL_W // POOL_GROUPS
IN_WIDTHS = (GLA_KEY_W, GLA_KEY_W, GLA_VAL_W, GLA_VAL_W, GLA_GATE_RANK, POOL_W, D_MODEL, D_MODEL)
D_IN = sum(IN_WIDTHS)
N_GROUPS = 4
EXPERTS_PER_GROUP = 8
N_EXPERTS = N_GROUPS * EXPERTS_PER_GROUP
TOP_K_IN_GROUP = 2
D_EXPERT = 256
MOE_BLOCK = 128
NORM_EPS = 1e-6


def rmsnorm_2(x, g):
    xf = x.astype(jnp.float32)
    y = xf * lax.rsqrt(jnp.mean(xf * xf, axis=-1, keepdims=True) + NORM_EPS)
    return (y * g.astype(jnp.float32)).astype(x.dtype)

def gla_mix(q, k, v, log_a):
    B, S, _ = q.shape
    C = GLA_CHUNK
    N = S // C

    def split(t, d):
        return t.astype(jnp.float32).reshape(B, N, C, GLA_HEADS, d).transpose(0, 3, 1, 2, 4)

    qc, kc, gc = split(q, GLA_DK), split(k, GLA_DK), split(log_a, GLA_DK)
    vc = split(v, GLA_DV)
    b = jnp.cumsum(gc, axis=3)
    b_last = b[:, :, :, -1:, :]
    q_dec = qc * jnp.exp(b) * (GLA_DK ** -0.5)
    k_dec = kc * jnp.exp(-b)
    causal = jnp.tril(jnp.ones((C, C), dtype=bool))
    scores = jnp.where(causal, jnp.einsum('bhntd,bhnsd->bhnts', q_dec, k_dec), 0.0)
    o_intra = jnp.einsum('bhnts,bhnsv->bhntv', scores, vc)
    k_end = kc * jnp.exp(b_last - b)
    inc = jnp.einsum('bhnsd,bhnsv->bhndv', k_end, vc)
    decay = jnp.exp(b_last[:, :, :, 0, :])

    def step(state, inp):
        dec, u = inp
        return dec[..., None] * state + u, state

    state0 = jnp.zeros((B, GLA_HEADS, GLA_DK, GLA_DV), jnp.float32)
    _, s_prev = lax.scan(step, state0, (jnp.moveaxis(decay, 2, 0), jnp.moveaxis(inc, 2, 0)))
    s_prev = jnp.moveaxis(s_prev, 0, 2)
    o = o_intra + jnp.einsum('bhntd,bhndv->bhntv', q_dec, s_prev)
    return o.transpose(0, 2, 3, 1, 4).reshape(B, S, GLA_VAL_W)

def head_rmsnorm(o, g):
    B, S, _ = o.shape
    oh = o.reshape(B, S, GLA_HEADS, GLA_DV)
    oh = oh * lax.rsqrt(jnp.mean(oh * oh, axis=-1, keepdims=True) + NORM_EPS)
    return oh.reshape(B, S, GLA_VAL_W) * g.astype(jnp.float32)

def pool_mix(u, pool_w, pool_scale):
    B, S, _ = u.shape
    uf = u.astype(jnp.float32)
    ug = uf.reshape(B, S, POOL_GROUPS, POOL_GW)
    cs = jnp.cumsum(uf, axis=1).reshape(B, S, POOL_GROUPS, POOL_GW)
    pos = jnp.arange(S, dtype=jnp.float32)
    pooled = []
    for gi, w in enumerate(POOL_WINDOWS):
        c = cs[:, :, gi]
        shifted = jnp.pad(c[:, :S - w], ((0, 0), (w, 0), (0, 0)))
        cnt = jnp.minimum(pos + 1.0, float(w))[None, :, None]
        pooled.append((c - shifted) / cnt)
    pooled = jnp.stack(pooled, axis=2)
    mixed = jnp.einsum('bsgc,gcd->bsgd', pooled - ug, pool_w.astype(jnp.float32))
    return (mixed.reshape(B, S, POOL_W) * pool_scale.astype(jnp.float32)).astype(u.dtype)

def hier_moe(h, w_rg, b_rg, w_re, b_re, w_gate, w_up, w_down):
    B, S, D = h.shape
    T = B * S
    ht = h.reshape(T, D)
    g_logits = (ht @ w_rg).astype(jnp.float32) + b_rg.astype(jnp.float32)
    g_p, g_idx = lax.top_k(jax.nn.softmax(g_logits, axis=-1), 1)
    e_all = jnp.einsum('td,gde->tge', ht, w_re).astype(jnp.float32) + b_re.astype(jnp.float32)
    e_logits = e_all[jnp.arange(T), g_idx[:, 0]]
    e_top, e_idx = lax.top_k(e_logits, TOP_K_IN_GROUP)
    gate = g_p * jax.nn.softmax(e_top, axis=-1)
    A = T * TOP_K_IN_GROUP
    weights = gate.reshape(A)
    expert_ids = (g_idx * EXPERTS_PER_GROUP + e_idx).reshape(A).astype(jnp.int32)
    token_ids = jnp.repeat(jnp.arange(T, dtype=jnp.int32), TOP_K_IN_GROUP)

    n_blocks = -(-(A + N_EXPERTS * (MOE_BLOCK - 1)) // MOE_BLOCK)
    R = n_blocks * MOE_BLOCK
    order = jnp.argsort(expert_ids)
    sorted_e = expert_ids[order]
    counts = jnp.zeros((N_EXPERTS,), jnp.int32).at[expert_ids].add(1)
    padded = ((counts + MOE_BLOCK - 1) // MOE_BLOCK) * MOE_BLOCK
    starts = jnp.cumsum(counts) - counts
    pends = jnp.cumsum(padded)
    pstarts = pends - padded
    dest = pstarts[sorted_e] + (jnp.arange(A, dtype=jnp.int32) - starts[sorted_e])
    row_token = jnp.full((R,), T, jnp.int32).at[dest].set(token_ids[order])
    row_w = jnp.zeros((R,), jnp.float32).at[dest].set(weights[order])
    block_e = jnp.minimum(jnp.searchsorted(pends, jnp.arange(n_blocks, dtype=jnp.int32) * MOE_BLOCK,
                                           side='right'), N_EXPERTS - 1).astype(jnp.int32)
    h_pad = jnp.concatenate([ht, jnp.zeros((1, D), ht.dtype)], axis=0)
    x_blocks = h_pad[row_token].reshape(n_blocks, MOE_BLOCK, D)

    def expert_block(args):
        xb, e = args
        return (jax.nn.silu(xb @ w_gate[e]) * (xb @ w_up[e])) @ w_down[e]

    y_rows = lax.map(expert_block, (x_blocks, block_e)).reshape(R, D)
    y_rows = y_rows * row_w[:, None].astype(y_rows.dtype)
    out = jnp.zeros((T + 1, D), y_rows.dtype).at[row_token].add(y_rows)[:T]
    return out.reshape(B, S, D).astype(h.dtype)

def second_inputs(seed: int = 0) -> dict:
    key = jax.random.key(seed)
    ks = jax.random.split(key, 24)
    L, D = DEPTH, D_MODEL
    nrm = lambda k, shape, s: jax.random.normal(k, shape, jnp.float32) * s
    return {
        "x": nrm(ks[0], (BATCH, SEQ, D), 1.0),
        "norm1_g": 1.0 + nrm(ks[1], (L, D), 0.05),
        "w_in": nrm(ks[2], (L, D, D_IN), D ** -0.5),
        "w_alpha_up": nrm(ks[3], (L, GLA_GATE_RANK, GLA_KEY_W), GLA_GATE_RANK ** -0.5),
        "b_alpha": nrm(ks[4], (L, GLA_KEY_W), 0.1),
        "gla_norm_g": 1.0 + nrm(ks[5], (L, GLA_VAL_W), 0.05),
        "w_gla_branch": nrm(ks[6], (L, GLA_VAL_W, D), GLA_VAL_W ** -0.5),
        "pool_w": nrm(ks[7], (L, POOL_GROUPS, POOL_GW, POOL_GW), POOL_GW ** -0.5),
        "pool_scale": 1.0 + nrm(ks[8], (L, POOL_W), 0.05),
        "w_pool_branch": nrm(ks[9], (L, POOL_W, D), POOL_W ** -0.5),
        "w_out": nrm(ks[10], (L, D, D), D ** -0.5),
        "norm2_g": 1.0 + nrm(ks[11], (L, D), 0.05),
        "w_router_group": nrm(ks[12], (L, D, N_GROUPS), D ** -0.5),
        "b_router_group": nrm(ks[13], (L, N_GROUPS), 0.01),
        "w_router_expert": nrm(ks[14], (L, N_GROUPS, D, EXPERTS_PER_GROUP), D ** -0.5),
        "b_router_expert": nrm(ks[15], (L, N_GROUPS, EXPERTS_PER_GROUP), 0.01),
        "w_exp_gate": nrm(ks[16], (L, N_EXPERTS, D, D_EXPERT), D ** -0.5),
        "w_exp_up": nrm(ks[17], (L, N_EXPERTS, D, D_EXPERT), D ** -0.5),
        "w_exp_down": nrm(ks[18], (L, N_EXPERTS, D_EXPERT, D), D_EXPERT ** -0.5),
        "norm_f_g": 1.0 + nrm(ks[19], (D,), 0.05),
    }

def second_block(x, norm1_g, w_in, w_alpha_up, b_alpha, gla_norm_g, w_gla_branch, pool_w, pool_scale,
              w_pool_branch, w_out, norm2_g, w_router_group, b_router_group, w_router_expert,
              b_router_expert, w_exp_gate, w_exp_up, w_exp_down, norm_f_g):
    split_idx = [int(i) for i in np.cumsum(IN_WIDTHS)[:-1]]
    for l in range(DEPTH):
        h = rmsnorm_2(x, norm1_g[l])
        proj = h @ w_in[l]
        q, k, v, r, a_low, u_pool, gate_gla, gate_pool = jnp.split(proj, split_idx, axis=-1)
        log_a = jax.nn.log_sigmoid((a_low @ w_alpha_up[l] + b_alpha[l]).astype(jnp.float32)) / GLA_GATE_NORMALIZER
        o = gla_mix(q, k, v, log_a)
        o = (head_rmsnorm(o, gla_norm_g[l]) * jax.nn.silu(r.astype(jnp.float32))).astype(x.dtype)
        y_gla = o @ w_gla_branch[l]
        y_pool = pool_mix(u_pool, pool_w[l], pool_scale[l]) @ w_pool_branch[l]
        merged = jax.nn.sigmoid(gate_gla) * y_gla + jax.nn.sigmoid(gate_pool) * y_pool
        x = x + merged @ w_out[l]
        h2 = rmsnorm_2(x, norm2_g[l])
        x = x + hier_moe(h2, w_router_group[l], b_router_group[l], w_router_expert[l], b_router_expert[l],
                         w_exp_gate[l], w_exp_up[l], w_exp_down[l])
    return rmsnorm_2(x, norm_f_g)


def setup_inputs(seed=0):
    out = dict(first_inputs(seed))
    for name, value in second_inputs(seed + 1).items():
        if name != "x":
            out[name + "_2"] = value
    return out


def reference(
    x, attn_pre_norm, w_in, forget_bias, swa_sinks, rel_bias, q_latent_norm, w_uq,
    kv_latent_norm, w_ukv, group_norm, w_out, attn_post_norm, ffn_pre_norm, w_up, conv_w,
    conv_b, w_down, ffn_post_norm, norm1_g_2, w_in_2, w_alpha_up_2, b_alpha_2, gla_norm_g_2,
    w_gla_branch_2, pool_w_2, pool_scale_2, w_pool_branch_2, w_out_2, norm2_g_2,
    w_router_group_2, b_router_group_2, w_router_expert_2, b_router_expert_2, w_exp_gate_2,
    w_exp_up_2, w_exp_down_2, norm_f_g_2,
):
    x = first_block(
        x, attn_pre_norm, w_in, forget_bias, swa_sinks, rel_bias, q_latent_norm, w_uq,
        kv_latent_norm, w_ukv, group_norm, w_out, attn_post_norm, ffn_pre_norm, w_up, conv_w,
        conv_b, w_down, ffn_post_norm,
    )
    return second_block(
        x, norm1_g_2, w_in_2, w_alpha_up_2, b_alpha_2, gla_norm_g_2, w_gla_branch_2, pool_w_2,
        pool_scale_2, w_pool_branch_2, w_out_2, norm2_g_2, w_router_group_2, b_router_group_2,
        w_router_expert_2, b_router_expert_2, w_exp_gate_2, w_exp_up_2, w_exp_down_2,
        norm_f_g_2,
    )


_drawn_inputs = setup_inputs


def setup_inputs(seed=0):
    import zlib

    import numpy as np

    out = dict(_drawn_inputs(seed))
    spreads = {}
    factors = {'swa_sinks': 3.383,
     'b_alpha_2': 4.084,
     'gla_norm_g_2': 3.243,
     'pool_scale_2': 3.422,
     'b_router_group_2': 17.685,
     'b_router_expert_2': 27.131,
     'norm2_g_2': 2.881}
    for name, (base, spread) in spreads.items():
        noise = np.random.default_rng([zlib.crc32(name.encode()), seed]).standard_normal(out[name].shape)
        drawn = base * np.exp(spread * noise) if base else spread * noise
        out[name] = __import__('jax').numpy.asarray(drawn.astype(out[name].dtype))
    for name, factor in factors.items():
        out[name] = (out[name] * factor).astype(out[name].dtype)
    return out
```

```python
import math
from contextlib import ExitStack

import numpy as np

import concourse.bass as bass
from concourse import mybir
from concourse.alu_op_type import AluOpType as ALU

P = 128
S = 256
TT = S // P
D = 1024
KD = D // P
HD = 64
SWA_HEADS, SWA_KV, FOX_HEADS, MLA_HEADS = 8, 2, 4, 4
HEADS = SWA_HEADS + FOX_HEADS + MLA_HEADS
WINDOW = 128
NOPE, ROPE = 64, 32
HALF = ROPE // 2
MLA_QK = NOPE + ROPE
Q_RANK, KV_RANK = 256, 128
BUCKETS, MAX_DIST = 32, 128
D_FF = 2816
FF_CHUNK = 256
FF_CHUNKS = D_FF // FF_CHUNK
FF_TILES = D_FF // P
EPS = 1e-6
NEG = -1e30
GLA_HEADS, GLA_DK, GLA_DV, GLA_RANK, GLA_CHUNK = 4, 64, 128, 16, 64
GLA_KEY, GLA_VAL = GLA_HEADS * GLA_DK, GLA_HEADS * GLA_DV
GATE_NORMALIZER = 16.0
POOL_WINDOWS = (2, 4, 8, 16)
POOL_G = len(POOL_WINDOWS)
PAD = max(POOL_WINDOWS)
GROUPS, PER_GROUP = 4, 8
EXPERTS = GROUPS * PER_GROUP
TOP_K = 2
SLOTS = S * TOP_K
SB = SLOTS // P
CH = 64
MORE = S // CH - 1
TASKS = SLOTS // CH
D_EXP = 256

RING = 6
UNIT = 2048
U_PROJ = 0
U_WOUT = U_PROJ + 8
U_FFN = U_WOUT + 4
U_GLA = U_FFN + 3 * FF_CHUNKS
U_BRANCH = U_GLA + 16
U_WOUT2 = U_BRANCH + 4
U_EXP = U_WOUT2 + 4
UNITS = U_EXP + 3 * EXPERTS


class Columns:

    def __init__(self):
        self.at, self.size = {}, 0

    def add(self, name, n):
        self.at[name] = (self.size, self.size + n)
        self.size += n

    def __getitem__(self, name):
        a, b = self.at[name]
        return slice(a, b)


CC = Columns()
for _n, _w in (("ident", P), ("tri", P), ("ones", P), ("stri", P), ("btri", P), ("causal", P + S),
               ("iota", SLOTS), ("cos", TT * HALF), ("sin", TT * HALF), ("rcount", POOL_G * PAD),
               ("bucket", P + S), ("line", P + S), ("foxq", FOX_HEADS * P), ("foxk", FOX_HEADS * S),
               ("units_of", 3 * EXPERTS * MORE), ("pass_of", EXPERTS * MORE)):
    CC.add(_n, _w)
VC = Columns()
for _n, _w in (("attn_pre", KD), ("group", KD), ("ffn_pre", KD), ("norm1", KD), ("norm2", KD),
               ("q_lat", Q_RANK // P), ("kv_lat", 1), ("pool_scale", POOL_G), ("gla", GLA_HEADS),
               ("conv", 3 * 2 * FF_TILES), ("conv_b", 2 * FF_TILES)):
    VC.add(_n, _w)
RC = Columns()
for _n, _w in (("attn_post", D), ("ffn_post", D), ("final", D), ("b_alpha", GLA_KEY),
               ("router_b", GROUPS + EXPERTS), ("forget", FOX_HEADS), ("sinks", SWA_HEADS)):
    RC.add(_n, _w)
SC = Columns()
for _n, _w in (("uq", 2 * MLA_HEADS * MLA_QK), ("ukv", MLA_HEADS * (NOPE + HD)), ("w_alpha", GLA_KEY),
               ("a_low", KD * GLA_RANK), ("router", KD * (GROUPS + EXPERTS)), ("pool_w", POOL_G * P),
               ("rel", SWA_HEADS)):
    SC.add(_n, _w)


class Chain:

    def __init__(self, engine, sem):
        self.engine, self.sem, self.n, self.extra = engine, sem, 0, 0

    def mark(self, instruction):
        instruction.then_inc(self.sem, 1)
        self.n += 1

    def sync(self):
        self.engine.wait_ge(self.sem, self.n + self.extra)

    def __call__(self, instruction):
        self.mark(instruction)
        self.sync()


def build(nc, x_in, units_in, const_in, vec_in, rows_in, small_in, out):
    fp32, i32 = mybir.dt.float32, mybir.dt.int32
    ACT = mybir.ActivationFunctionType
    AX = mybir.AxisListType
    MUL, ADD, SUB, MAX, MIN, EQ, GT = ALU.mult, ALU.add, ALU.subtract, ALU.max, ALU.min, ALU.is_equal, ALU.is_gt
    ds = bass.ds
    mm = nc.tensor.matmul

    results_dram = nc.dram_tensor("results_scratch", [SLOTS + CH, D], fp32, kind="Internal").ap()
    line_dram = nc.dram_tensor("line_scratch", [SWA_HEADS, P, P + S], fp32, kind="Internal").ap()

    ctx = ExitStack()
    with ctx:
        def sb(name, shape, dt=fp32):
            return ctx.enter_context(nc.sbuf_tensor(name, shape, dt))

        def sem(name):
            return ctx.enter_context(nc.semaphore(name))

        ring = sb("ring", [P, RING, UNIT])
        const = sb("const", [P, CC.size])
        vec = sb("vec", [P, VC.size])
        rows = sb("rows", [P, RC.size])
        small = sb("small", [P, SC.size])
        X = sb("X", [P, TT, D])
        HN = sb("HN", [P, TT, D])
        HT = sb("HT", [P, KD, S])
        junk = sb("junk", [P, D])
        ss = sb("ss", [P, 10, 8])
        ms = sb("ms", [P, 10, 8])
        rstd = sb("rstd", [P, 10, 8])
        neghalf = sb("neghalf", [P, 8])
        ARENA = 22600
        arena = sb("arena", [P, ARENA])
        starti = sb("starti", [P, EXPERTS], i32)
        taski = sb("taski", [P, 4 * TASKS + 1], i32)
        psum = ctx.enter_context(nc.psum_tensor("psum", [P, 8, 512], fp32))

        class Arena:

            def __init__(self):
                self.at = 0

            def tile(self, *dims):
                n = math.prod(dims)
                v = arena[:, self.at:self.at + n]
                self.at += n
                assert self.at <= ARENA, self.at
                if len(dims) == 1:
                    return v
                names = "abcd"[:len(dims)]
                return v.rearrange(f"p ({' '.join(names)}) -> p {' '.join(names)}",
                                   **{k: d for k, d in zip(names[1:], dims[1:])})

        def c_(name):
            return const[:, CC[name]]

        def v_(name, i):
            a = VC[name].start + i
            return vec[:, a:a + 1]

        def r_(name):
            return rows[:, RC[name]]

        def s_(name):
            return small[:, SC[name]]

        ident, ones, tri, stri, btri = c_("ident"), c_("ones"), c_("tri"), c_("stri"), c_("btri")
        causal, iota = c_("causal"), c_("iota")

        A = Arena()
        bias = A.tile(SWA_HEADS, P + S)
        line = A.tile(P + S)
        QA, KA, VA = A.tile(4, S), A.tile(S), A.tile(TT, P)
        QF, KF, VF = A.tile(2, S), A.tile(2, S), A.tile(TT, 256)
        CQ, CK = A.tile(TT, Q_RANK), A.tile(TT, 164)
        CQT, CKT = A.tile(2, S), A.tile(S)
        QM, KM = A.tile(TT, MLA_HEADS, MLA_QK), A.tile(TT, MLA_HEADS, MLA_QK)
        VM = A.tile(TT, MLA_HEADS, HD)
        QMT, KMT = A.tile(MLA_HEADS, S), A.tile(MLA_HEADS, S)
        QR = A.tile(TT, MLA_HEADS + 1, ROPE)
        rot = A.tile(4, TT, (MLA_HEADS + 1) * HALF)
        FT = A.tile(S)
        fz, fabs, fexp, flog, flf = (A.tile(TT, FOX_HEADS) for _ in range(5))
        NS = 3
        SM = A.tile(NS, P + S + 2)
        PT = A.tile(2, 3, P)
        O = A.tile(TT, D)
        nmax, psums, rsum = A.tile(HEADS, 2), A.tile(HEADS, 2), A.tile(HEADS, 2)
        A = Arena()
        U = A.tile(2, 4, S)
        G = A.tile(2, 2, S)
        AF = A.tile(2, 2, S)
        T2 = A.tile(TT, D)
        A = Arena()
        AL = A.tile(S)
        SP = arena[:, A.at:A.at + KD * S].rearrange("p (a b) -> p a b", a=KD)
        z2, zabs, zexp, LA = A.tile(TT, GLA_KEY), A.tile(TT, GLA_KEY), A.tile(TT, GLA_KEY), A.tile(TT, GLA_KEY)
        BC, EB, ENB, KE = A.tile(2, S), A.tile(2, S), A.tile(2, S), A.tile(2, S)
        DEC = A.tile(2, 4)
        QD, KDE, KEND = A.tile(2, S), A.tile(2, S), A.tile(2, S)
        QZ = A.tile(2, TT, 2, P)
        KET, V = A.tile(TT, GLA_KEY), A.tile(TT, GLA_VAL)
        ST = A.tile(TT, GLA_HEADS, P)
        SS = A.tile(3, 2, S)
        OHN, OT = A.tile(TT, GLA_VAL), A.tile(4, S)
        UP, PA, PB = A.tile(POOL_G, PAD + S), A.tile(POOL_G, PAD + S), A.tile(POOL_G, PAD + S)
        PM, YP, RS = A.tile(POOL_G, S), A.tile(POOL_G, S), A.tile(4, S)
        SG = A.tile(KD, S)
        T1a, T1b = A.tile(2, S), A.tile(2, S)
        A = Arena()
        NR = GROUPS + EXPERTS
        LG = A.tile(TT, NR)
        EM, EQX, CAND, OH1, OH2, M, RK, PR = (A.tile(TT, EXPERTS) for _ in range(8))
        g4a, g4b, g4c, g4d = (A.tile(TT, GROUPS) for _ in range(4))
        col = A.tile(16, TT)
        CNT, CUM, START = A.tile(EXPERTS), A.tile(EXPERTS), A.tile(EXPERTS)
        NJ = EXPERTS * MORE
        MF, MC, MS, MB, onesrow = (A.tile(NJ) for _ in range(5))
        TASK = A.tile(4, TASKS)
        PG, WP, WQ = A.tile(TT, SLOTS), A.tile(TT, SLOTS), A.tile(TT, SLOTS)
        TOH, TMUL = A.tile(TASKS, NJ), A.tile(TASKS, NJ)
        CT = A.tile(SB, S)
        XS = A.tile(KD, SLOTS + CH)
        XW = A.tile(2, KD, CH)
        SL, AT = A.tile(2, D_EXP), A.tile(2, D_EXP)
        AE = A.tile(2, 2, CH)
        YO = A.tile(2, D)
        YS = A.tile(SB, D)

        x_loaded, const_loaded, vec_loaded, rows_loaded, small_loaded = map(
            sem, ("x_loaded", "const_loaded", "vec_loaded", "rows_loaded", "small_loaded"))
        unit_loaded = [sem(f"unit_loaded{i}") for i in range(RING)]
        unit_used = sem("unit_used")
        squares_summed, ms_ready, rstd_ready = map(sem, ("squares_summed", "ms_ready", "rstd_ready"))
        hn_dve, hn_act, tr_done, ht_dve, ht_act = map(sem, ("hn_dve", "hn_act", "tr_done", "ht_dve", "ht_act"))
        x_ready, y_done = sem("x_ready"), sem("y_done")
        line_done, line_sb, line_stored, bias_loaded = map(
            sem, ("line_done", "line_sb", "line_stored", "bias_loaded"))
        evac_dve, evac_act = sem("evac_dve"), sem("evac_act")
        lat_hn, lat_tr, lat_ct, lat_up, q_split, qk_rot, qk_tr, qmt_sb, kmt_sb = map(
            sem, ("lat_hn", "lat_tr", "lat_ct", "lat_up", "q_split", "qk_rot", "qk_tr", "qmt_sb", "kmt_sb"))
        fz_ready, flog_ready, flf_ready, ft_done, ft_sb = map(
            sem, ("fz_ready", "flog_ready", "flf_ready", "ft_done", "ft_sb"))
        s_done, s_read, mx_ready, exp_done, pt_done, pt_sb, pv_done, o_sb = map(
            sem, ("s_done", "s_read", "mx_ready", "exp_done", "pt_done", "pt_sb", "pv_done", "o_sb"))
        tap_last, gate_conv, gelu_done, act_ready = map(
            sem, ("tap_last", "gate_conv", "gelu_done", "act_ready"))
        al_done, al_sb, z_done, z_abs, z_log, la_ready, bc_done, bc_sb, exps_done = map(
            sem, ("al_done", "al_sb", "z_done", "z_abs", "z_log", "la_ready", "bc_done", "bc_sb", "exps_done"))
        g_dve, g_act, kend_tr, kend_sb, v_sb, st_done, st_sb, inc_done, states_ready, o_done, ohn_ready = map(
            sem, ("g_dve", "g_act", "kend_tr", "kend_sb", "v_sb", "st_done", "st_sb", "inc_done",
                  "states_ready", "o_done", "ohn_ready"))
        ot_tr, ot_sb, pool_in, pool_sums, pm_ready, pool_done, yp_sb, merged = map(
            sem, ("ot_tr", "ot_sb", "pool_in", "pool_sums", "pm_ready", "pool_done", "yp_sb", "merged"))
        lg_done, top_in, top_exp, top_e, top_eexp, m_ready, rank_done, pg_ready, wp_ready = map(
            sem, ("lg_done", "top_in", "top_exp", "top_e", "top_eexp", "m_ready", "rank_done", "pg_ready",
                  "wp_ready"))
        tasks_ready = sem("tasks_ready")
        xs_done, xs_dve, xs_act, ct_done, ct_sb = map(sem, ("xs_done", "xs_dve", "xs_act", "ct_done", "ct_sb"))
        pad_zero, starts_ready, xw_ready, silu_done, at_ready, at_tr, ae_ready, y_copied, y_stored = map(
            sem, ("pad_zero", "starts_ready", "xw_ready", "silu_done", "at_ready", "at_tr", "ae_ready",
                  "y_copied", "y_stored"))
        more_loaded, more_xw, more_up, more_silu, more_at, more_tr, more_ae, more_copied, more_stored = map(
            sem, ("more_loaded", "more_xw", "more_up", "more_silu", "more_at", "more_tr", "more_ae",
                  "more_copied", "more_stored"))
        ys_loaded = [sem(f"ys_loaded{s}") for s in range(SB)]
        out_ready, out_stored, final_x = sem("out_ready"), sem("out_stored"), sem("final_x")
        up_conv, pool_zero = sem("up_conv"), sem("pool_zero")
        dve_steps, act_steps, pool_steps = sem("dve_steps"), sem("act_steps"), sem("pool_steps")

        block = ctx.enter_context(nc.Block())

        def unit(engine, n, i=0):
            engine.wait_ge(unit_loaded[n % RING], 16 * (n // RING + 1) + 16 * i)
            return ring[:, n % RING, :]

        def proj_bank(i):
            return psum[:, i % 8, :].rearrange("p (a b) -> p a b", a=2)

        @block.sync
        def _(sp):
            sp.dma_start(X[:, :, :], x_in).then_inc(x_loaded, 16)
            sp.dma_start(const[:, :], const_in).then_inc(const_loaded, 16)
            sp.dma_start(vec[:, :], vec_in).then_inc(vec_loaded, 16)
            sp.dma_start(small[:, :], small_in).then_inc(small_loaded, 16)
            for n in range(RING):
                sp.dma_start(ring[:, n, :], units_in[n]).then_inc(unit_loaded[n], 16)
                if n == 1:
                    sp.dma_start(rows[:, :], rows_in.to_broadcast([P, RC.size])).then_inc(rows_loaded, 16)
            rounds = (UNITS - RING) // RING
            with sp.Fori(0, rounds) as i:
                for k in range(RING):
                    sp.wait_ge(unit_used, i * RING + (k + 1))
                    sp.dma_start(ring[:, k, :], units_in[ds(i * RING + (RING + k), 1)]
                                 .rearrange("a p n -> p (a n)")).then_inc(unit_loaded[k], 16)
            for n in range(RING + rounds * RING, UNITS):
                sp.wait_ge(unit_used, n - RING + 1)
                sp.dma_start(ring[:, n % RING, :], units_in[n]).then_inc(unit_loaded[n % RING], 16)

            sp.wait_ge(tasks_ready, 1)
            total = sp.value_load(taski[0:1, 4 * TASKS:4 * TASKS + 1], min_val=0, max_val=TASKS)
            with sp.If(total > 0):
                with sp.Fori(0, total) as t:
                    sp.wait_ge(unit_used, t + UNITS)
                    for k in range(3):
                        u = sp.value_load(taski[0:1, ds(t + k * TASKS, 1)], min_val=0, max_val=UNITS - 1)
                        sp.dma_start(ring[:, k, :], units_in[ds(u, 1)]
                                     .rearrange("a p n -> p (a n)")).then_inc(more_loaded, 16)
                sp.nop()
            sp.nop()
            for tt in range(TT):
                sp.wait_ge(out_ready, tt + 1)
                sp.dma_start(out[tt], HN[:, tt, :]).then_inc(out_stored, 16)
            sp.wait_ge(out_stored, 16 * TT)

        @block.tensor
        def _(pe):
            def transposes(stage):
                pe.wait_ge(hn_dve, stage + 1)
                pe.wait_ge(hn_act, stage + 1)
                for b in range(KD // 2):
                    for k in range(2):
                        for tt in range(TT):
                            at = k * S + tt * P
                            last = nc.tensor.transpose(psum[:, b, at:at + P],
                                                       HN[:, tt, (2 * b + k) * P:(2 * b + k + 1) * P], ident)
                    last.then_inc(tr_done, 1)

            def ht_ready(stage):
                pe.wait_ge(ht_dve, stage + 1)
                pe.wait_ge(ht_act, stage + 1)

            def features(bank, w, half, stride=FF_CHUNK):
                for k in range(KD):
                    last = mm(psum[:, bank, half * S:half * S + S], w[:, k * stride + half * P:k * stride + half * P + P],
                              HT[:, k, :], start=k == 0, stop=k == KD - 1)
                return last

            def tokens(bank, w, a, n, at):
                for tt in range(TT):
                    for k in range(KD):
                        last = mm(psum[:, bank, tt * S + at:tt * S + at + n] if n != P else
                                  psum[:, bank, at + tt * P:at + tt * P + n],
                                  HT[:, k, tt * P:(tt + 1) * P], w[:, k * FF_CHUNK + a:k * FF_CHUNK + a + n],
                                  start=k == 0, stop=k == KD - 1)
                return last

            def rows_out(n0, count, lhs):
                for j in range(count):
                    w = unit(pe, n0 + j)
                    for kk in range(2):
                        for tt in range(TT):
                            for n in range(2):
                                last = mm(psum[:, 4 + 2 * tt + n, :], lhs[:, 2 * j + kk, tt * P:(tt + 1) * P],
                                          w[:, kk * D + n * 512:kk * D + n * 512 + 512],
                                          start=j == 0 and kk == 0, stop=j == count - 1 and kk == 1)
                    last.then_inc(unit_used, 1)

            pe.wait_ge(const_loaded, 16)
            pe.wait_ge(small_loaded, 16)
            mm(psum[0:SWA_HEADS, 4, 0:P + S], s_("rel")[0:BUCKETS, :], c_("bucket")[0:BUCKETS, :],
               start=True, stop=True).then_inc(line_done, 1)

            transposes(0)
            ht_ready(0)
            pe.wait_ge(line_sb, 1)
            for i in range(8):
                w = unit(pe, U_PROJ + i)
                if i == 0:
                    last = tokens(0, w, 0, 256, 0)
                elif i == 1:
                    last = tokens(1, w, 0, 164, 0)
                elif i == 2:
                    last = tokens(2, w, 0, 256, 0)
                elif i == 3:
                    features(3, w, 0)
                    last = tokens(3, w, P, P, S)
                else:
                    features(i, w, 0)
                    last = features(i, w, 1)
                last.then_inc(unit_used, 1)

            pe.wait_ge(lat_hn, 1)
            for tt in range(TT):
                for k in range(2):
                    nc.tensor.transpose(psum[:, 0, k * S + tt * P:k * S + tt * P + P], CQ[:, tt, k * P:(k + 1) * P],
                                        ident)
            for tt in range(TT):
                last = nc.tensor.transpose(psum[:, 1, tt * P:(tt + 1) * P], CK[:, tt, 0:P], ident)
            last.then_inc(lat_tr, 1)
            pe.wait_ge(flf_ready, 1)
            pe.wait_ge(evac_dve, 4)
            mm(psum[0:FOX_HEADS, 6, 0:S], flf[:, 0, :], const[:, CC["tri"].start:CC["ones"].stop],
               start=True, stop=False)
            mm(psum[0:FOX_HEADS, 6, P:S], flf[:, 1, :], tri, start=False, stop=True).then_inc(ft_done, 1)
            pe.wait_ge(lat_ct, 1)
            pe.wait_ge(evac_act, 4)
            uq = s_("uq").rearrange("p (k n) -> p k n", k=2)
            for tt in range(TT):
                for k in range(2):
                    mm(psum[:, 2 + tt, 0:MLA_HEADS * MLA_QK], CQT[:, k, tt * P:(tt + 1) * P], uq[:, k, :],
                       start=k == 0, stop=k == 1)
                last = mm(psum[:, 4 + tt, :], CKT[:, tt * P:(tt + 1) * P], s_("ukv"), start=True, stop=True)
            last.then_inc(lat_up, 1)
            pe.wait_ge(qk_rot, 1)
            for tt in range(TT):
                for h in range(MLA_HEADS):
                    nc.tensor.transpose(psum[0:MLA_QK, tt, h * P:(h + 1) * P], QM[:, tt, h, :], ident)
                    last = nc.tensor.transpose(psum[0:MLA_QK, 2 + tt, h * P:(h + 1) * P], KM[:, tt, h, :], ident)
            last.then_inc(qk_tr, 1)
            pe.wait_ge(ft_sb, 1)
            pe.wait_ge(qmt_sb, 1)
            pe.wait_ge(kmt_sb, 1)

            def logits(h):
                if h >= 2:
                    pe.wait_ge(s_read, h - 1)
                for qb in range(TT):
                    o = psum[:, 4 + h % 2, 0:P] if qb == 0 else psum[:, 4 + h % 2, P:P + S]
                    nk = P * (qb + 1)
                    q_at = slice(qb * P, (qb + 1) * P)
                    if h < SWA_HEADS:
                        kv, base = h // 4, HD * (h // 4)
                        last = mm(o, QA[base:base + HD, h % 4, q_at], KA[base:base + HD, 0:nk], start=True, stop=True)
                    elif h < SWA_HEADS + FOX_HEADS:
                        f = h - SWA_HEADS
                        base = HD * (f % 2)
                        mm(o, QF[base:base + HD, f // 2, q_at], KF[base:base + HD, f // 2, 0:nk],
                           start=True, stop=False)
                        mm(o, FT[0:FOX_HEADS, q_at], c_("foxk")[0:FOX_HEADS, f * S:f * S + nk],
                           start=False, stop=False)
                        last = mm(o, c_("foxq")[0:FOX_HEADS, f * P:(f + 1) * P], FT[0:FOX_HEADS, 0:nk],
                                  start=False, stop=True)
                    else:
                        m = h - SWA_HEADS - FOX_HEADS
                        last = mm(o, QMT[0:MLA_QK, m, q_at], KMT[0:MLA_QK, m, 0:nk], start=True, stop=True)
                last.then_inc(s_done, 1)

            def value_tile(h, tt):
                if h < SWA_HEADS:
                    return VA[:, tt, HD * (h // 4):HD * (h // 4) + HD]
                if h < SWA_HEADS + FOX_HEADS:
                    return VF[:, tt, HD * (h - SWA_HEADS):HD * (h - SWA_HEADS) + HD]
                return VM[:, tt, h - SWA_HEADS - FOX_HEADS, :]

            logits(0)
            logits(1)
            for h in range(HEADS):
                pe.wait_ge(exp_done, h + 1)
                if h >= 2:
                    pe.wait_ge(pt_sb, h - 1)
                for b in range(3):
                    last = nc.tensor.transpose(psum[:, 6 + h % 2, b * P:(b + 1) * P],
                                               SM[:, h % NS, 1 + b * P:1 + (b + 1) * P], ident)
                last.then_inc(pt_done, 1)
                if h + 2 < HEADS:
                    logits(h + 2)
                pe.wait_ge(pt_sb, h + 1)
                if h % 4 == 0 and h >= 8:
                    pe.wait_ge(o_sb, h // 4 - 1)
                o = psum[:, 2 + (h // 4) % 2, (h % 4) * P:(h % 4 + 1) * P]
                mm(o[:, 0:HD], PT[:, h % 2, 0, :], value_tile(h, 0), start=True, stop=True)
                mm(o[:, HD:P], PT[:, h % 2, 1, :], value_tile(h, 0), start=True, stop=False)
                mm(o[:, HD:P], PT[:, h % 2, 2, :], value_tile(h, 1), start=False, stop=True).then_inc(pv_done, 1)

            transposes(1)
            ht_ready(1)
            rows_out(U_WOUT, 4, HT)

            transposes(2)
            ht_ready(2)

            def ffn_up(c, n0, i=0):
                for g in range(2):
                    w = unit(pe, n0 + g, i)
                    features(2 * (c % 2) + g, w, 0)
                    features(2 * (c % 2) + g, w, 1).then_inc(unit_used, 1)

            def ffn_down(c, n0, i=0, ready=None, first=False, final=False):
                pe.wait_ge(act_ready, ready)
                w = unit(pe, n0, i)
                for kk in range(2):
                    for tt in range(TT):
                        for n in range(2):
                            last = mm(psum[:, 4 + 2 * tt + n, :], AF[:, c % 2, kk, tt * P:(tt + 1) * P],
                                      w[:, kk * D + n * 512:kk * D + n * 512 + 512],
                                      start=first and kk == 0, stop=final and kk == 1)
                last.then_inc(unit_used, 1)

            ffn_up(0, U_FFN)
            for c in range(2):
                ffn_up(c + 1, U_FFN + 2 + 3 * c)
                ffn_down(c, U_FFN + 4 + 3 * c, ready=c + 1, first=c == 0)
            with pe.Fori(0, (FF_CHUNKS - 3) // 2) as i:
                for c in (2, 3):
                    ffn_up(c + 1, U_FFN + 2 + 3 * c, i)
                    ffn_down(c, U_FFN + 4 + 3 * c, i, ready=i * 2 + (c + 1))
            ffn_down(FF_CHUNKS - 1, U_FFN + 3 * FF_CHUNKS - 1, ready=FF_CHUNKS, final=True)

            transposes(3)
            ht_ready(3)
            al = s_("a_low").rearrange("p (k n) -> p k n", k=KD)
            for k in range(KD):
                last = mm(psum[0:GLA_RANK, 4, 0:S], al[:, k, :], HT[:, k, :], start=k == 0, stop=k == KD - 1)
            last.then_inc(al_done, 1)

            def gla_unit(j, bank, major=features):
                w = unit(pe, U_GLA + j)
                if major is tokens:
                    last = tokens(bank, w, 0, 256, 0)
                else:
                    features(bank, w, 0)
                    last = features(bank, w, 1)
                last.then_inc(unit_used, 1)

            gla_unit(0, 0)
            pe.wait_ge(al_sb, 1)
            for tt in range(TT):
                last = mm(psum[:, 5, tt * S:(tt + 1) * S], AL[0:GLA_RANK, tt * P:(tt + 1) * P],
                          s_("w_alpha")[0:GLA_RANK, :], start=True, stop=True)
            last.then_inc(z_done, 1)
            gla_unit(1, 1)
            gla_unit(2, 2, tokens)
            gla_unit(3, 3, tokens)
            pe.wait_ge(la_ready, 1)
            for f in range(2):
                for tt in range(TT):
                    last = mm(psum[:, 4, f * S + tt * P:f * S + (tt + 1) * P], LA[:, tt, f * P:(f + 1) * P], btri,
                              start=True, stop=True)
            last.then_inc(bc_done, 1)
            gla_unit(4, 6)
            gla_unit(5, 7)
            pe.wait_ge(g_dve, 2)
            for tt in range(TT):
                for f in range(2):
                    last = nc.tensor.transpose(psum[:, 0, tt * S + f * P:tt * S + (f + 1) * P],
                                               KEND[:, f, tt * P:(tt + 1) * P], ident)
            last.then_inc(kend_tr, 1)
            for odd in range(2):
                base = HD * odd
                for tt in range(TT):
                    for f in range(2):
                        at = (2 * tt + f) * P
                        last = mm(psum[:, (1, 4)[odd], at:at + P], KDE[base:base + HD, f, tt * P:(tt + 1) * P],
                                  QD[base:base + HD, f, tt * P:(tt + 1) * P], start=True, stop=True)
                last.then_inc(st_done, 1)
            pe.wait_ge(kend_sb, 1)
            pe.wait_ge(v_sb, 2)
            pe.wait_ge(z_abs, 1)
            for n in range(3):
                base = HD * (n % 2)
                b = (2, 3, 5)[n]
                for f in range(2):
                    last = mm(psum[:, b, f * S:(f + 1) * S], KET[base:base + HD, n // 2, f * P:(f + 1) * P],
                              V[base:base + HD, n // 2, f * S:(f + 1) * S], start=True, stop=True)
                last.then_inc(inc_done, 1)
            pe.wait_ge(st_sb, 2)
            pe.wait_ge(states_ready, 3)
            for odd in range(2):
                base = HD * odd
                for tt in range(TT):
                    for f in range(2):
                        h = 2 * f + odd
                        o = psum[:, (1, 4)[odd], (2 * tt + f) * P:(2 * tt + f + 1) * P]
                        chunks = [2 * tt + c for c in range(2) if 2 * tt + c > 0]
                        mm(o, ST[:, tt, h, :], V[:, tt, h * P:(h + 1) * P], start=True, stop=False)
                        for n in chunks:
                            last = mm(o, QZ[base:base + HD, f, tt, n % 2, :],
                                      SS[base:base + HD, n - 1, f, odd * P:(odd + 1) * P],
                                      start=False, stop=n == chunks[-1])
                last.then_inc(o_done, 1)
            pe.wait_ge(pool_in, 2)
            gla_unit(6, 6)
            gla_unit(7, 7)
            for j in range(4):
                gla_unit(8 + j, (2, 3, 0, 5)[j])
            pe.wait_ge(pm_ready, 1)
            pe.wait_ge(g_act, 2)
            pw = s_("pool_w").rearrange("p (g n) -> p g n", g=POOL_G)
            for g in range(POOL_G):
                last = mm(psum[:, 6 + g // 2, (g % 2) * S:(g % 2 + 1) * S], pw[:, g, :], PM[:, g, :],
                          start=True, stop=True)
            last.then_inc(pool_done, 1)
            pe.wait_ge(ohn_ready, 2)
            for k in range(4):
                for tt in range(TT):
                    last = nc.tensor.transpose(psum[:, (1, 4)[k // 2], (k % 2) * S + tt * P:(k % 2) * S + (tt + 1) * P],
                                               OHN[:, tt, k * P:(k + 1) * P], ident)
            last.then_inc(ot_tr, 1)
            pe.wait_ge(g_act, 6)
            for j in range(4):
                gla_unit(12 + j, (2, 3, 0, 5)[j])
            pe.wait_ge(ot_sb, 1)
            pe.wait_ge(yp_sb, 1)
            for j in range(2):
                if j == 1:
                    pe.wait_ge(merged, 2)
                for src, b0 in ((OT, (6, 7)), (YP, (1, 4))):
                    w = unit(pe, U_BRANCH + 2 * j + (src is YP))
                    for m in range(4):
                        for k in range(4):
                            last = mm(psum[:, b0[m // 2], (m % 2) * S:(m % 2 + 1) * S],
                                      w[:, k * 512 + m * P:k * 512 + (m + 1) * P], src[:, k, :],
                                      start=k == 0, stop=k == 3)
                    last.then_inc(unit_used, 1)
            pe.wait_ge(merged, 4)
            rows_out(U_WOUT2, 4, HT)

            transposes(4)
            ht_ready(4)
            wr = s_("router").rearrange("p (k n) -> p k n", k=KD)
            for tt in range(TT):
                for k in range(KD):
                    last = mm(psum[:, 4, tt * NR:(tt + 1) * NR], HT[:, k, tt * P:(tt + 1) * P], wr[:, k, :],
                              start=k == 0, stop=k == KD - 1)
            last.then_inc(lg_done, 1)
            pe.wait_ge(m_ready, 1)
            mm(psum[:, 5, 0:EXPERTS], stri, M[:, 0, :], start=True, stop=True)
            mm(psum[:, 5, EXPERTS:2 * EXPERTS], ones, M[:, 0, :], start=True, stop=False)
            mm(psum[:, 5, EXPERTS:2 * EXPERTS], stri, M[:, 1, :], start=False, stop=True)
            mm(psum[:, 5, 2 * EXPERTS:3 * EXPERTS], ones, M[:, 0, :], start=True, stop=False)
            mm(psum[:, 5, 2 * EXPERTS:3 * EXPERTS], ones, M[:, 1, :], start=False, stop=True).then_inc(rank_done, 1)
            pe.wait_ge(pg_ready, 1)
            for m in range(KD):
                if m >= 4:
                    pe.wait_ge(xs_dve, (m - 4) // 2 + 1)
                    pe.wait_ge(xs_act, (m - 4 + 1) // 2)
                for tt in range(TT):
                    last = mm(psum[:, m % 4, :], HN[:, tt, m * P:(m + 1) * P], PG[:, tt, :],
                              start=tt == 0, stop=tt == TT - 1)
                last.then_inc(xs_done, 1)
            pe.wait_ge(wp_ready, 1)
            for s in range(SB):
                for tt in range(TT):
                    last = nc.tensor.transpose(psum[:, 6 + s // 2, (s % 2) * S + tt * P:(s % 2) * S + (tt + 1) * P],
                                               WP[:, tt, s * P:(s + 1) * P], ident)
            last.then_inc(ct_done, 1)
            pe.wait_ge(ct_sb, 1)

            def expert_up(par, g, w, ks=range(KD)):
                for k in ks:
                    last = mm(psum[0:CH, par, g * D_EXP:(g + 1) * D_EXP], XW[:, par, k, :],
                              w[:, k * D_EXP:(k + 1) * D_EXP], start=k == 0, stop=k == KD - 1)
                return last

            def expert_turn(par):
                for f in range(2):
                    last = nc.tensor.transpose(psum[:, 4 + par, f * CH:(f + 1) * CH], AT[0:CH, par, f * P:(f + 1) * P],
                                               ident[0:CH, 0:CH])
                return last

            def expert_down(par, w):
                for n in range(2):
                    for f in range(2):
                        last = mm(psum[0:CH, (2, 6)[par] + n, :], AE[:, par, f, :],
                                  w[:, f * D + n * 512:f * D + (n + 1) * 512], start=f == 0, stop=f == 1)
                return last

            def experts(e, i=0):
                if e < EXPERTS - 1:
                    pe.wait_ge(xw_ready, i * 2 + (e + 2))
                    expert_up((e + 1) % 2, 0, unit(pe, U_EXP + 2 + 3 * e, i)).then_inc(unit_used, 1)
                    w = unit(pe, U_EXP + 3 + 3 * e, i)
                pe.wait_ge(at_ready, i * 2 + (e + 1))
                if e < EXPERTS - 1:
                    expert_up((e + 1) % 2, 1, w, range(1))
                expert_turn(e % 2).then_inc(at_tr, 1)
                if e < EXPERTS - 1:
                    expert_up((e + 1) % 2, 1, w, range(1, KD)).then_inc(unit_used, 1)
                pe.wait_ge(ae_ready, i * 2 + (e + 1))
                if e >= 2:
                    pe.wait_ge(y_copied, i * 2 + (e - 1))
                expert_down(e % 2, unit(pe, U_EXP + 4 + 3 * e if e < EXPERTS - 1 else UNITS - 1, i)
                            ).then_inc(unit_used, 1)

            pe.wait_ge(xw_ready, 1)
            for g in range(2):
                expert_up(0, g, unit(pe, U_EXP + g)).then_inc(unit_used, 1)
            experts(0)
            experts(1)
            with pe.Fori(0, (EXPERTS - 4) // 2) as i:
                experts(2, i)
                experts(3, i)
            experts(EXPERTS - 2)
            experts(EXPERTS - 1)

            pe.wait_ge(tasks_ready, 1)
            total = pe.value_load(taski[0:1, 4 * TASKS:4 * TASKS + 1], min_val=0, max_val=TASKS)
            with pe.If(total > 0):
                pe.wait_ge(y_copied, EXPERTS - 1)
                with pe.Fori(0, total) as t:
                    pe.wait_ge(more_loaded, t * 48 + 48)
                    pe.wait_ge(more_xw, t + 1)
                    expert_up(0, 0, ring[:, 0, :])
                    expert_up(0, 1, ring[:, 1, :]).then_inc(more_up, 1)
                    pe.wait_ge(tasks_ready, 1)
                    pe.wait_ge(more_at, t + 1)
                    expert_turn(0).then_inc(more_tr, 1)
                    pe.wait_ge(more_ae, t + 1)
                    expert_down(0, ring[:, 2, :]).then_inc(unit_used, 1)
                    pe.wait_ge(more_copied, t + 1)
                pe.nop()
            pe.nop()

            pe.wait_ge(y_copied, EXPERTS - 1)
            for s in range(SB):
                pe.wait_ge(ys_loaded[s], 16)
                for tt in range(TT):
                    for n in range(2):
                        last = mm(psum[:, 2 * tt + n, :], CT[:, s, tt * P:(tt + 1) * P],
                                  YS[:, s, n * 512:(n + 1) * 512], start=s == 0, stop=s == SB - 1)
            last.then_inc(y_done, 1)

        @block.scalar
        def _(act):
            step = Chain(act, act_steps)

            def sum_squares(event, parts):
                act.wait_ge(squares_summed, event)
                at = 0
                for n, part in enumerate(parts):
                    size = part.free_size()
                    if at + size > D:
                        step.sync()
                        at = 0
                    last = nc.scalar.activation(junk[:, at:at + size], part, ACT.Square,
                                                accum_out=ss[:, event, n:n + 1])
                    at += size
                    if n < len(parts) - 1:
                        step.mark(last)
                last.then_inc(squares_summed, 1)

            def norm(event, stage):
                sum_squares(event, [X[:, tt, :] for tt in range(TT)])
                act.wait_ge(rstd_ready, event + 1)
                nc.scalar.activation(HN[:, 1, :], X[:, 1, :], ACT.Copy, scale=rstd[:, event, 1:2]).then_inc(hn_act, 1)

            def take_transposes(stage, gain):
                for b in (1, 3):
                    act.wait_ge(tr_done, 4 * stage + b + 1)
                    for k in range(2):
                        last = nc.scalar.activation(HT[:, 2 * b + k, :], psum[:, b, k * S:(k + 1) * S], ACT.Copy,
                                                    scale=v_(gain, 2 * b + k))
                last.then_inc(ht_act, 1)

            def copy(out_, in_):
                return nc.scalar.activation(out_, in_, ACT.Copy)

            act.wait_ge(x_loaded, 16)
            norm(0, 0)
            act.wait_ge(vec_loaded, 16)
            take_transposes(0, "attn_pre")

            act.wait_ge(unit_used, U_PROJ + 3)
            copy(VF, proj_bank(2)).then_inc(evac_act, 1)
            act.wait_ge(evac_dve, 2)
            sum_squares(1, [CQ[:, 0, :], CQ[:, 1, :], CK[:, 0, 0:P], CK[:, 1, 0:P]])
            act.wait_ge(unit_used, U_PROJ + 4)
            copy(KA, psum[:, 3, 0:S])
            copy(VA, psum[:, 3, S:2 * S].rearrange("p (a b) -> p a b", a=TT)).then_inc(evac_act, 1)
            act.wait_ge(unit_used, U_PROJ + 6)
            copy(QA[:, 2:4, :], proj_bank(5)).then_inc(evac_act, 1)
            act.wait_ge(fz_ready, 1)
            step(nc.scalar.activation(fexp, fabs, ACT.Exp, scale=-1.0))
            nc.scalar.activation(flog, fexp, ACT.Ln, bias=1.0).then_inc(flog_ready, 1)
            act.wait_ge(unit_used, U_PROJ + 8)
            copy(KF, proj_bank(7)).then_inc(evac_act, 1)
            act.wait_ge(lat_up, 1)
            for tt in range(TT):
                q = psum[:, 2 + tt, 0:MLA_HEADS * MLA_QK].rearrange("p (h n) -> p h n", h=MLA_HEADS)
                copy(QM[:, tt, :, 0:NOPE], q[:, :, 0:NOPE])
                last = copy(QR[:, tt, 0:MLA_HEADS, :], q[:, :, NOPE:MLA_QK])
            last.then_inc(q_split, 1)
            act.wait_ge(qk_tr, 1)
            for tt in range(TT):
                last = copy(KMT[0:MLA_QK, :, tt * P:(tt + 1) * P],
                            psum[0:MLA_QK, 2 + tt, :].rearrange("p (h n) -> p h n", h=MLA_HEADS))
            last.then_inc(kmt_sb, 1)

            for h in range(HEADS):
                act.wait_ge(mx_ready, h + 1)
                nc.scalar.activation(SM[:, h % NS, 0:P + 1], SM[:, h % NS, 0:P + 1], ACT.Exp,
                                     bias=nmax[:, h, 0:1], accum_out=psums[:, h, 0:1])
                nc.scalar.activation(SM[:, h % NS, P + 1:P + S + 2], SM[:, h % NS, P + 1:P + S + 2], ACT.Exp,
                                     bias=nmax[:, h, 1:2], accum_out=psums[:, h, 1:2]).then_inc(exp_done, 1)

            act.wait_ge(o_sb, HEADS // 4)
            spans = (slice(0, 512), slice(512, 768), slice(768, 1024))
            sum_squares(2, [O[:, tt, sp_] for sp_ in spans for tt in range(TT)])
            act.wait_ge(rstd_ready, 3)
            for g, sp_ in enumerate(spans):
                last = nc.scalar.activation(HN[:, 1, sp_], O[:, 1, sp_], ACT.Copy, scale=rstd[:, 2, 2 * g + 1:2 * g + 2])
            last.then_inc(hn_act, 1)
            take_transposes(1, "group")
            act.wait_ge(unit_used, U_FFN)
            sum_squares(3, [psum[:, 4 + 2 * tt:6 + 2 * tt, :].rearrange("p a b -> p (a b)") for tt in range(TT)])

            act.wait_ge(x_ready, 1)
            norm(4, 2)
            take_transposes(2, "ffn_pre")
            c0, cb = VC["conv"].start, VC["conv_b"].start

            def ffn_taps(par, tile, used, gates):
                act.wait_ge(unit_used, used)
                for g in range(2):
                    for f in range(2):
                        at = tile + (g * FF_TILES + f)
                        last = nc.scalar.activation(
                            U[:, par, 2 * g + f, :], psum[:, 2 * par + g, f * S:(f + 1) * S], ACT.Identity,
                            bias=vec[:, ds(at + cb, 1)], scale=vec[:, ds(at + (c0 + 2 * 2 * FF_TILES), 1)])
                    last.then_inc(tap_last, 1)
                act.wait_ge(gate_conv, gates)
                nc.scalar.activation(G[:, par], U[:, par, 0:2, :], ACT.Gelu_apprx_tanh).then_inc(gelu_done, 1)

            ffn_taps(0, 0, U_FFN + 2, 1)
            ffn_taps(1, 2, U_FFN + 4, 2)
            with act.Fori(0, (FF_CHUNKS - 3) // 2) as i:
                for c in (2, 3):
                    ffn_taps(c % 2, i * 4 + 2 * c, i * 6 + (U_FFN + 3 * c + 1), i * 2 + (c + 1))
            ffn_taps(0, 2 * (FF_CHUNKS - 1), U_FFN + 3 * (FF_CHUNKS - 1) + 1, FF_CHUNKS)
            act.wait_ge(unit_used, U_GLA)
            sum_squares(5, [psum[:, 4 + 2 * tt:6 + 2 * tt, :].rearrange("p a b -> p (a b)") for tt in range(TT)])

            act.wait_ge(x_ready, 2)
            norm(6, 3)
            take_transposes(3, "norm1")
            act.wait_ge(al_done, 1)
            copy(AL[0:GLA_RANK, :], psum[0:GLA_RANK, 4, 0:S]).then_inc(al_sb, 1)
            act.wait_ge(z_abs, 1)
            step(nc.scalar.activation(zexp, zabs, ACT.Exp, scale=-1.0))
            nc.scalar.activation(zabs, zexp, ACT.Ln, bias=1.0).then_inc(z_log, 1)
            for j in range(2):
                act.wait_ge(unit_used, U_GLA + 3 + j)
                copy(V[:, :, j * S:(j + 1) * S], proj_bank(2 + j)).then_inc(v_sb, 1)
            act.wait_ge(bc_done, 1)
            step.mark(copy(BC, psum[:, 4, :].rearrange("p (a b) -> p a b", a=2)))
            nc.scalar.activation(EB, psum[:, 4, :].rearrange("p (a b) -> p a b", a=2), ACT.Exp)
            nc.scalar.activation(ENB, psum[:, 4, :].rearrange("p (a b) -> p a b", a=2), ACT.Exp, scale=-1.0)
            step.sync()
            for f in range(2):
                for n in range(S // GLA_CHUNK):
                    a, b = n * GLA_CHUNK, (n + 1) * GLA_CHUNK
                    nc.scalar.activation(KE[:, f, a:b], BC[:, f, a:b], ACT.Exp, bias=BC[:, f, b - 1:b], scale=-1.0)
                last = nc.scalar.activation(DEC[:, f, :], BC[:, f, GLA_CHUNK - 1:S:GLA_CHUNK], ACT.Exp)
            last.then_inc(exps_done, 1)
            for j in range(2):
                act.wait_ge(unit_used, U_GLA + 5 + j)
                copy(UP[:, 2 * j:2 * j + 2, PAD:PAD + S], proj_bank(6 + j)).then_inc(pool_in, 1)
            act.wait_ge(kend_tr, 1)
            copy(KET, proj_bank(0)).then_inc(kend_sb, 1)
            act.wait_ge(o_done, 2)
            sum_squares(7, [psum[:, b, n * P:(n + 1) * P] for b in (1, 4) for n in range(4)])
            for j in range(2):
                act.wait_ge(unit_used, U_GLA + 7 + j)
                nc.scalar.activation(RS[:, 2 * j:2 * j + 2, :], proj_bank(6 + j), ACT.Silu).then_inc(g_act, 1)
            for dst, first in ((SG, 8), (SP, 12)):
                for j in range(4):
                    act.wait_ge(unit_used, U_GLA + first + j + 1)
                    nc.scalar.activation(dst[:, 2 * j:2 * j + 2, :], proj_bank((2, 3, 0, 5)[j]),
                                         ACT.Sigmoid).then_inc(g_act, 1)

            act.wait_ge(x_ready, 3)
            norm(8, 4)
            take_transposes(4, "norm2")
            act.wait_ge(top_in, 1)
            nc.scalar.activation(g4b, g4a, ACT.Exp).then_inc(top_exp, 1)
            act.wait_ge(top_e, 1)
            nc.scalar.activation(col[:, 4, :], col[:, 3, :], ACT.Exp).then_inc(top_eexp, 1)
            for m in (1, 3, 5, 7):
                act.wait_ge(xs_done, m + 1)
                nc.scalar.activation(XS[:, m, 0:SLOTS], psum[:, m % 4, :], ACT.Copy,
                                     scale=v_("norm2", m)).then_inc(xs_act, 1)

            def window(par, at):
                return copy(XW[:, par], XS[:, :, ds(at, CH)])

            def silu(par):
                return nc.scalar.activation(SL[0:CH, par], psum[0:CH, par, 0:D_EXP], ACT.Silu)

            def experts(e, i=0):
                act.wait_ge(unit_used, i * 6 + (U_EXP + 2 if e == 0 else U_EXP + 1 + 3 * e))
                silu(e % 2).then_inc(silu_done, 1)
                if e < EXPERTS - 2:
                    at = act.value_load(starti[0:1, ds(i * 2 + (e + 2), 1)], min_val=0, max_val=SLOTS)
                    window(e % 2, at).then_inc(xw_ready, 1)

            act.wait_ge(pad_zero, 1)
            act.wait_ge(xs_dve, 4)
            act.wait_ge(xs_act, 4)
            act.wait_ge(starts_ready, 1)
            for e in range(2):
                at = act.value_load(starti[0:1, e:e + 1], min_val=0, max_val=SLOTS)
                window(e, at).then_inc(xw_ready, 1)
            experts(0)
            experts(1)
            with act.Fori(0, (EXPERTS - 4) // 2) as i:
                experts(2, i)
                experts(3, i)
            experts(EXPERTS - 2)
            experts(EXPERTS - 1)

            act.wait_ge(tasks_ready, 1)
            total = act.value_load(taski[0:1, 4 * TASKS:4 * TASKS + 1], min_val=0, max_val=TASKS)
            with act.If(total > 0):
                with act.Fori(0, total) as t:
                    at = act.value_load(taski[0:1, ds(t + 3 * TASKS, 1)], min_val=0, max_val=SLOTS)
                    window(0, at).then_inc(more_xw, 1)
                    act.wait_ge(more_up, t + 1)
                    silu(0).then_inc(more_silu, 1)
                act.nop()
            act.nop()
            act.wait_ge(final_x, 1)
            sum_squares(9, [X[:, tt, :] for tt in range(TT)])

        @block.gpsimd
        def _(pool):
            nc.gpsimd.memset(neghalf[:, :], -0.5).then_inc(pool_steps, 1)
            pool.wait_ge(pool_steps, 1)
            steps = 1

            def inverse_roots(event, n):
                pool.wait_ge(ms_ready, event + 1)
                nc.gpsimd.tensor_tensor(rstd[:, event, 0:n], ms[:, event, 0:n], neghalf[:, 0:n],
                                        ALU.pow).then_inc(rstd_ready, 1)

            inverse_roots(0, 2)
            pool.wait_ge(line_sb, 1)
            pool.dma_start(line_dram, line[0:SWA_HEADS, :].unsqueeze(1).to_broadcast([SWA_HEADS, P, P + S])
                           ).then_inc(line_stored, 16)
            pool.wait_ge(line_stored, 16)
            for a, n, first in ((0, P, P + P - 1), (P, S, P - 1)):
                src = bass.AP(line_dram.tensor, first, [[P + S - 1, P], [P * (P + S), SWA_HEADS], [1, n]])
                pool.dma_start(bias[:, :, a:a + n], src).then_inc(bias_loaded, 16)
            for event, n in ((1, 4), (2, 6), (3, 2), (4, 2), (5, 2), (6, 2)):
                inverse_roots(event, n)
            pool.wait_ge(pool_zero, 1)
            pool.wait_ge(pool_in, 2)
            t0 = PAD
            for n, (dst, src, g) in enumerate(((PA, UP, 0), (PB, PA, 1), (PA, PB, 2), (PB, PA, 3))):
                shift = 1 << n
                last = nc.gpsimd.tensor_tensor(dst[:, g:, t0:], src[:, g:, t0:], src[:, g:, t0 - shift:PAD + S - shift],
                                               ADD)
                if n < 3:
                    last.then_inc(pool_steps, 1)
                    steps += 1
                    pool.wait_ge(pool_steps, steps)
            last.then_inc(pool_sums, 1)
            for event, n in ((7, 8), (8, 2)):
                inverse_roots(event, n)

            def experts(e, i=0):
                at = pool.value_load(starti[0:1, ds(i * 2 + e, 1)], min_val=0, max_val=SLOTS)
                pool.wait_ge(y_copied, i * 2 + (e + 1))
                if e >= 1:
                    pool.wait_ge(y_stored, i * 32 + 16 * e)
                pool.dma_start(results_dram[ds(at, CH)], YO[0:CH, e % 2, :]).then_inc(y_stored, 16)

            pool.wait_ge(starts_ready, 1)
            experts(0)
            experts(1)
            with pool.Fori(0, (EXPERTS - 2) // 2) as i:
                experts(2, i)
                experts(3, i)
            pool.wait_ge(y_stored, 16 * EXPERTS)

            pool.wait_ge(tasks_ready, 1)
            total = pool.value_load(taski[0:1, 4 * TASKS:4 * TASKS + 1], min_val=0, max_val=TASKS)
            with pool.If(total > 0):
                with pool.Fori(0, total) as t:
                    at = pool.value_load(taski[0:1, ds(t + 3 * TASKS, 1)], min_val=0, max_val=SLOTS)
                    pool.wait_ge(more_copied, t + 1)
                    pool.dma_start(results_dram[ds(at, CH)], YO[0:CH, 0, :]).then_inc(more_stored, 16)
                    pool.wait_ge(more_stored, t * 16 + 16)
                pool.nop()
            pool.nop()
            for s in range(SB):
                pool.dma_start(YS[:, s, :], results_dram[s * P:(s + 1) * P]).then_inc(ys_loaded[s], 16)
            inverse_roots(9, 2)

        @block.vector
        def _(dve):
            step = Chain(dve, dve_steps)
            V_ = nc.vector
            tt_op, ts_op, stt = V_.tensor_tensor, V_.tensor_scalar, V_.scalar_tensor_tensor

            def mean_squares(event, parts):
                dve.wait_ge(squares_summed, event + 1)
                for a, b, n in parts:
                    last = ts_op(ms[:, event, a:b], ss[:, event, a:b], 1.0 / n, EPS, MUL, ADD)
                last.then_inc(ms_ready, 1)
                dve.wait_ge(rstd_ready, event + 1)

            def norm(event):
                mean_squares(event, [(0, 2, D)])
                ts_op(HN[:, 0, :], X[:, 0, :], rstd[:, event, 0:1], None, MUL).then_inc(hn_dve, 1)

            def take_transposes(stage, gain):
                for b in (0, 2):
                    dve.wait_ge(tr_done, 4 * stage + b + 1)
                    for k in range(2):
                        last = ts_op(HT[:, 2 * b + k, :], psum[:, b, k * S:(k + 1) * S], v_(gain, 2 * b + k), None, MUL)
                last.then_inc(ht_dve, 1)

            def add_branch(event, row):
                mean_squares(event, [(0, 2, D)])
                for tt in range(TT):
                    step.mark(stt(T2[:, tt, :], psum[:, 4 + 2 * tt:6 + 2 * tt, :].rearrange("p a b -> p (a b)"),
                                  rstd[:, event, tt:tt + 1], r_(row), MUL, MUL))
                step.sync()
                for tt in range(TT):
                    last = tt_op(X[:, tt, :], X[:, tt, :], T2[:, tt, :], ADD)
                last.then_inc(x_ready, 1)

            dve.wait_ge(x_loaded, 16)
            norm(0)
            dve.wait_ge(vec_loaded, 16)
            take_transposes(0, "attn_pre")
            dve.wait_ge(const_loaded, 16)
            dve.wait_ge(line_done, 1)
            tt_op(line[0:SWA_HEADS, :], psum[0:SWA_HEADS, 4, 0:P + S], c_("line")[0:SWA_HEADS, :], ADD).then_inc(line_sb, 1)

            dve.wait_ge(unit_used, U_PROJ + 1)
            V_.tensor_copy(CQ, proj_bank(0)).then_inc(evac_dve, 1)
            dve.wait_ge(unit_used, U_PROJ + 2)
            V_.tensor_copy(CK, proj_bank(1)[:, :, 0:164]).then_inc(evac_dve, 1)
            dve.wait_ge(evac_dve, 2)
            dve.wait_ge(rows_loaded, 16)
            step(tt_op(fz, CK[:, :, 160:164], r_("forget").unsqueeze(1).to_broadcast([P, TT, FOX_HEADS]), ADD))
            stt(fabs, fz, -1.0, fz, MUL, MAX).then_inc(fz_ready, 1)
            mean_squares(1, [(0, 2, Q_RANK), (2, 4, KV_RANK)])
            for tt in range(TT):
                ts_op(CQ[:, tt, :], CQ[:, tt, :], rstd[:, 1, tt:tt + 1], None, MUL)
                last = ts_op(CK[:, tt, 0:P], CK[:, tt, 0:P], rstd[:, 1, 2 + tt:3 + tt], None, MUL)
            last.then_inc(lat_hn, 1)
            dve.wait_ge(unit_used, U_PROJ + 5)
            V_.tensor_copy(QA[:, 0:2, :], proj_bank(4)).then_inc(evac_dve, 1)
            dve.wait_ge(flog_ready, 1)
            stt(flf, fz, 0.0, flog, MIN, SUB).then_inc(flf_ready, 1)
            dve.wait_ge(unit_used, U_PROJ + 7)
            V_.tensor_copy(QF, proj_bank(6)).then_inc(evac_dve, 1)
            dve.wait_ge(lat_tr, 1)
            for k in range(2):
                ts_op(CQT[:, k, :], psum[:, 0, k * S:(k + 1) * S], v_("q_lat", k), None, MUL)
            ts_op(CKT, psum[:, 1, 0:S], v_("kv_lat", 0), None, MUL).then_inc(lat_ct, 1)
            dve.wait_ge(ft_done, 1)
            V_.tensor_copy(FT[0:FOX_HEADS, :], psum[0:FOX_HEADS, 6, 0:S]).then_inc(ft_sb, 1)
            V_.tensor_copy(QR[:, :, MLA_HEADS, :], CK[:, :, P:P + ROPE])
            dve.wait_ge(lat_up, 1)
            for tt in range(TT):
                kv = psum[:, 4 + tt, :].rearrange("p (h n) -> p h n", h=MLA_HEADS)
                V_.tensor_copy(KM[:, tt, :, 0:NOPE], kv[:, :, 0:NOPE])
                last = V_.tensor_copy(VM[:, tt], kv[:, :, NOPE:])
            step(last)
            dve.wait_ge(q_split, 1)
            nh = MLA_HEADS + 1
            lo, hi = QR[:, :, :, 0:HALF], QR[:, :, :, HALF:ROPE]
            r4 = [rot[:, q].rearrange("p t (h n) -> p t h n", h=nh) for q in range(4)]
            cs, sn = (c_(k).rearrange("p (t n) -> p t n", t=TT).unsqueeze(2).to_broadcast([P, TT, nh, HALF])
                      for k in ("cos", "sin"))
            for q, (part, trig) in enumerate(((lo, cs), (hi, sn), (lo, sn), (hi, cs))):
                step.mark(tt_op(r4[q], part, trig, MUL))
            step.sync()
            for n, (x1, x2, op) in enumerate(((r4[0], r4[1], SUB), (r4[2], r4[3], ADD))):
                at = NOPE + n * HALF
                tt_op(QM[:, :, :, at:at + HALF], x1[:, :, 0:MLA_HEADS], x2[:, :, 0:MLA_HEADS], op)
                for tt in range(TT):
                    last = tt_op(KM[:, tt, :, at:at + HALF],
                                 x1[:, tt, MLA_HEADS:nh].to_broadcast([P, MLA_HEADS, HALF]),
                                 x2[:, tt, MLA_HEADS:nh].to_broadcast([P, MLA_HEADS, HALF]), op)
            last.then_inc(qk_rot, 1)
            dve.wait_ge(qk_tr, 1)
            for tt in range(TT):
                last = V_.tensor_copy(QMT[0:MLA_QK, :, tt * P:(tt + 1) * P],
                                      psum[0:MLA_QK, tt, :].rearrange("p (h n) -> p h n", h=MLA_HEADS))
            last.then_inc(qmt_sb, 1)

            def take_probs(h):
                dve.wait_ge(pt_done, h + 1)
                if h >= 2:
                    dve.wait_ge(pv_done, h - 1)
                V_.tensor_copy(PT[:, h % 2], psum[:, 6 + h % 2, 0:3 * P].rearrange("p (a b) -> p a b", a=3)).then_inc(pt_sb, 1)

            def take_outputs(g):
                dve.wait_ge(pv_done, 4 * g + 4)
                step(V_.reciprocal(rsum[:, 4 * g:4 * g + 4, :], psums[:, 4 * g:4 * g + 4, :]))
                src = psum[:, 2 + g % 2, :].rearrange("p (h t n) -> p h t n", h=4, t=TT)
                for tt in range(TT):
                    last = tt_op(O[:, tt, 4 * g * HD:(4 * g + 4) * HD].rearrange("p (h n) -> p h n", h=4), src[:, :, tt, :],
                                 rsum[:, 4 * g:4 * g + 4, tt:tt + 1].to_broadcast([P, 4, HD]), MUL)
                last.then_inc(o_sb, 1)

            dve.wait_ge(bias_loaded, 32)
            for h in range(HEADS):
                b = SM[:, h % NS, :]
                if h >= NS:
                    dve.wait_ge(pt_done, h - NS + 1)
                ends = b[:, 0:P + S + 2:P + S + 1]
                if h < SWA_HEADS:
                    V_.tensor_copy(ends, r_("sinks")[:, h:h + 1].to_broadcast([P, 2]))
                else:
                    V_.memset(ends, NEG)
                dve.wait_ge(s_done, h + 1)
                scale = HD ** -0.5 if h < SWA_HEADS + FOX_HEADS else MLA_QK ** -0.5
                stt(b[:, 1:P + S + 1], psum[:, 4 + h % 2, 0:P + S], scale, bias[:, h, :] if h < SWA_HEADS else causal,
                    MUL, ADD).then_inc(s_read, 1)
                dve.wait_ge(s_read, h + 1)
                V_.tensor_reduce(nmax[:, h, 0:1], b[:, 0:P + 1], AX.X, MAX, negate=True)
                V_.tensor_reduce(nmax[:, h, 1:2], b[:, P + 1:P + S + 2], AX.X, MAX, negate=True).then_inc(mx_ready, 1)
                if h >= 1:
                    take_probs(h - 1)
                if h % 4 == 1 and h >= 5:
                    take_outputs(h // 4 - 1)
            take_probs(HEADS - 1)
            take_outputs(HEADS // 4 - 1)

            mean_squares(2, [(0, 2, 512), (2, 6, 256)])
            dve.wait_ge(o_sb, HEADS // 4)
            for g, (a, b) in enumerate(((0, 512), (512, 768), (768, 1024))):
                last = ts_op(HN[:, 0, a:b], O[:, 0, a:b], rstd[:, 2, 2 * g:2 * g + 1], None, MUL)
            last.then_inc(hn_dve, 1)
            take_transposes(1, "group")
            add_branch(3, "attn_post")

            dve.wait_ge(x_ready, 1)
            norm(4)
            take_transposes(2, "ffn_pre")
            c0 = VC["conv"].start

            def ffn_conv(par, tile, taps, gelus):
                for g in range(2):
                    dve.wait_ge(tap_last, taps + g)
                    for back in (1, 2):
                        for f in range(2):
                            at = tile + (g * FF_TILES + f)
                            u = U[:, par, 2 * g + f, back:S]
                            ins = stt(u, psum[:, 2 * par + g, f * S:(f + 1) * S - back],
                                      vec[:, ds(at + (c0 + (2 - back) * 2 * FF_TILES), 1)], u, MUL, ADD)
                            if back == 2 and f == 1:
                                ins.then_inc(gate_conv if g == 0 else up_conv, 1)
                            else:
                                step.mark(ins)
                        if back == 1:
                            step.sync()
                dve.wait_ge(gelu_done, gelus)
                dve.wait_ge(up_conv, gelus)
                tt_op(AF[:, par], G[:, par], U[:, par, 2:4, :], MUL).then_inc(act_ready, 1)

            ffn_conv(0, 0, 1, 1)
            ffn_conv(1, 2, 3, 2)
            at0 = step.n
            with dve.Fori(0, (FF_CHUNKS - 3) // 2) as i:
                step.extra = i * 12
                for c in (2, 3):
                    ffn_conv(c % 2, i * 4 + 2 * c, i * 4 + (2 * c + 1), i * 2 + (c + 1))
                assert step.n - at0 == 12
            step.n, step.extra = at0 + 12 * ((FF_CHUNKS - 3) // 2), 0
            ffn_conv(0, 2 * (FF_CHUNKS - 1), 2 * FF_CHUNKS - 1, FF_CHUNKS)
            add_branch(5, "ffn_post")

            dve.wait_ge(x_ready, 2)
            norm(6)
            take_transposes(3, "norm1")
            V_.memset(QZ, 0.0)
            V_.memset(ST, 0.0)
            for t_ in (UP, PA, PB):
                last = V_.memset(t_[:, :, 0:PAD], 0.0)
            last.then_inc(pool_zero, 1)
            dve.wait_ge(pool_zero, 1)
            dve.wait_ge(z_done, 1)
            step(tt_op(z2, psum[:, 5, :].rearrange("p (a b) -> p a b", a=TT),
                       r_("b_alpha").unsqueeze(1).to_broadcast([P, TT, GLA_KEY]), ADD))
            stt(zabs, z2, -1.0, z2, MUL, MAX).then_inc(z_abs, 1)
            dve.wait_ge(z_log, 1)
            step(stt(z2, z2, 0.0, zabs, MIN, SUB))
            ts_op(LA, z2, 1.0 / GATE_NORMALIZER, None, MUL).then_inc(la_ready, 1)
            dve.wait_ge(exps_done, 1)
            dve.wait_ge(unit_used, U_GLA + 2)
            step(stt(QD, proj_bank(0), GLA_DK ** -0.5, EB, MUL, MUL))
            for c in range(2):
                a = c * GLA_CHUNK
                last = V_.tensor_copy(QZ[:, :, :, c, a:a + GLA_CHUNK],
                                      QD.rearrange("p f (t n) -> p f t n", t=TT)[:, :, :, a:a + GLA_CHUNK])
            last.then_inc(g_dve, 1)
            tt_op(KDE, proj_bank(1), ENB, MUL)
            tt_op(KEND, proj_bank(1), KE, MUL).then_inc(g_dve, 1)
            mask = btri.bitcast(i32).unsqueeze(1).to_broadcast([P, 2, P])
            for odd in range(2):
                dve.wait_ge(st_done, odd + 1)
                for tt in range(TT):
                    last = V_.copy_predicated(ST[:, tt, odd::2, :], mask,
                                              psum[:, (1, 4)[odd], tt * S:(tt + 1) * S].rearrange("p (f n) -> p f n", f=2))
                last.then_inc(st_sb, 1)
            for n in range(3):
                dve.wait_ge(inc_done, n + 1)
                for f in range(2):
                    inc = psum[:, (2, 3, 5)[n], f * S:(f + 1) * S]
                    if n == 0:
                        last = V_.tensor_copy(SS[:, 0, f, :], inc)
                    else:
                        last = stt(SS[:, n, f, :], SS[:, n - 1, f, :], DEC[:, f, n:n + 1], inc, MUL, ADD)
                last.then_inc(states_ready, 1)
                dve.wait_ge(states_ready, n + 1)
            mean_squares(7, [(0, 8, GLA_DV)])
            for odd in range(2):
                for tt in range(TT):
                    at = 4 * odd + 2 * tt
                    last = tt_op(OHN[:, tt, :].rearrange("p (h n) -> p h n", h=GLA_HEADS)[:, odd::2, :],
                                 psum[:, (1, 4)[odd], tt * S:(tt + 1) * S].rearrange("p (f n) -> p f n", f=2),
                                 rstd[:, 7, at:at + 2].unsqueeze(2).to_broadcast([P, 2, P]), MUL)
                last.then_inc(ohn_ready, 1)
            dve.wait_ge(pool_sums, 1)
            for g, w in enumerate(POOL_WINDOWS):
                src = PA if g % 2 == 0 else PB
                stt(PM[:, g, PAD:], src[:, g, 2 * PAD:], 1.0 / w, UP[:, g, 2 * PAD:], MUL, SUB)
                step.mark(tt_op(PM[:, g, 0:PAD], src[:, g, PAD:2 * PAD],
                                c_("rcount").rearrange("p (g n) -> p g n", g=POOL_G)[:, g, :], MUL))
            step.sync()
            tt_op(PM[:, :, 0:PAD], PM[:, :, 0:PAD], UP[:, :, PAD:2 * PAD], SUB).then_inc(pm_ready, 1)
            dve.wait_ge(pool_done, 1)
            for g in range(POOL_G):
                last = ts_op(YP[:, g, :], psum[:, 6 + g // 2, (g % 2) * S:(g % 2 + 1) * S], v_("pool_scale", g), None, MUL)
            last.then_inc(yp_sb, 1)
            dve.wait_ge(ot_tr, 1)
            dve.wait_ge(g_act, 2)
            for k in range(4):
                last = stt(OT[:, k, :], psum[:, (1, 4)[k // 2], (k % 2) * S:(k % 2 + 1) * S], v_("gla", k),
                           RS[:, k, :], MUL, MUL)
            last.then_inc(ot_sb, 1)
            dve.wait_ge(g_act, 10)
            for j in range(2):
                dve.wait_ge(unit_used, U_BRANCH + 2 * j + 2)
                for hf in range(2):
                    m = 4 * j + 2 * hf
                    step.mark(tt_op(T1a, proj_bank(6 + hf), SG[:, m:m + 2, :], MUL))
                    step(tt_op(T1b, proj_bank((1, 4)[hf]), SP[:, m:m + 2, :], MUL))
                    tt_op(HT[:, m:m + 2, :], T1a, T1b, ADD).then_inc(merged, 1)
                    dve.wait_ge(merged, 2 * j + hf + 1)
            dve.wait_ge(unit_used, U_EXP)
            for tt in range(TT):
                last = tt_op(X[:, tt, :], X[:, tt, :], psum[:, 4 + 2 * tt:6 + 2 * tt, :].rearrange("p a b -> p (a b)"), ADD)
            last.then_inc(x_ready, 1)

            dve.wait_ge(x_ready, 3)
            norm(8)
            take_transposes(4, "norm2")
            dve.wait_ge(lg_done, 1)
            step(tt_op(LG, psum[:, 4, 0:TT * NR].rearrange("p (a b) -> p a b", a=TT),
                       r_("router_b").unsqueeze(1).to_broadcast([P, TT, NR]), ADD))

            def by_group(v):
                return v.rearrange("p (g e) -> p g e", g=GROUPS)

            def spread(v, n):
                return v.unsqueeze(2).to_broadcast([P, TT, n])

            def first_max(onehot, eq, cand, values, maximum, index, n):
                step(V_.tensor_reduce(maximum, values, AX.X, MAX))
                step(tt_op(eq, values, spread(maximum, n), EQ))
                step(stt(cand, eq, -1000.0, iota[:, 0:n].unsqueeze(1).to_broadcast([P, TT, n]), MUL, ADD))
                step(V_.tensor_reduce(index, cand, AX.X, MIN))
                step(tt_op(onehot, cand, spread(index, n), EQ))

            gmax, gidx, e1, dlt, ex, gp, den, w1, w2, e2, idx, d1, d2 = (col[:, n, :] for n in
                                                                         (0, 1, 2, 3, 4, 5, 6, 7, 8, 9, 10, 11, 12))
            first_max(g4d, g4b, g4c, LG[:, :, 0:GROUPS], gmax, gidx, GROUPS)
            tt_op(g4a, LG[:, :, 0:GROUPS], spread(gmax, GROUPS), SUB).then_inc(top_in, 1)
            for tt in range(TT):
                step.mark(tt_op(by_group(EM[:, tt]), by_group(LG[:, tt, GROUPS:NR]),
                                g4d[:, tt, :].unsqueeze(2).to_broadcast([P, GROUPS, PER_GROUP]), MUL))
            step(ts_op(g4c, g4d, 1.0, -NEG, SUB, MUL))
            for tt in range(TT):
                step.mark(tt_op(by_group(EM[:, tt]), by_group(EM[:, tt]),
                                g4c[:, tt, :].unsqueeze(2).to_broadcast([P, GROUPS, PER_GROUP]), ADD))
            step.sync()
            first_max(OH1, EQX, CAND, EM, e1, idx, EXPERTS)
            step(stt(EM, OH1, 2 * NEG, EM, MUL, ADD))
            first_max(OH2, EQX, CAND, EM, e2, idx, EXPERTS)
            tt_op(M, OH1, OH2, ADD).then_inc(m_ready, 1)
            tt_op(dlt, e2, e1, SUB).then_inc(top_e, 1)
            dve.wait_ge(top_exp, 1)
            step(V_.tensor_reduce(gp, g4b, AX.X, ADD))
            dve.wait_ge(top_eexp, 1)
            step(ts_op(den, ex, 1.0, None, ADD))
            step(tt_op(den, den, gp, MUL))
            step(V_.reciprocal(w1, den))
            step(tt_op(w2, w1, ex, MUL))

            dve.wait_ge(rank_done, 1)
            step(V_.tensor_copy(CNT, psum[:, 5, 2 * EXPERTS:3 * EXPERTS]))
            step(V_.tensor_tensor_scan(CUM, ones[:, 0:EXPERTS], CNT, 0.0, MUL, ADD))
            step(tt_op(START, CUM, CNT, SUB))
            step(tt_op(RK, psum[:, 5, 0:2 * EXPERTS].rearrange("p (a b) -> p a b", a=TT),
                       START.unsqueeze(1).to_broadcast([P, TT, EXPERTS]), ADD))
            for oh, d in ((OH1, d1), (OH2, d2)):
                step(tt_op(PR, oh, RK, MUL))
                step(V_.tensor_reduce(d, PR, AX.X, ADD))
            for tt in range(TT):
                step.mark(ts_op(PG[:, tt, :], iota, d1[:, tt:tt + 1], None, EQ))
            step.sync()
            for tt in range(TT):
                last = stt(PG[:, tt, :], iota, d2[:, tt:tt + 1], PG[:, tt, :], EQ, ADD)
            last.then_inc(pg_ready, 1)
            for tt in range(TT):
                step.mark(ts_op(WP[:, tt, :], iota, d1[:, tt:tt + 1], w1[:, tt:tt + 1], EQ, MUL))
                step.mark(ts_op(WQ[:, tt, :], iota, d2[:, tt:tt + 1], w2[:, tt:tt + 1], EQ, MUL))
            step.sync()
            tt_op(WP, WP, WQ, ADD).then_inc(wp_ready, 1)
            V_.memset(XS[:, :, SLOTS:], 0.0).then_inc(pad_zero, 1)
            V_.tensor_copy(starti[:, :], START).then_inc(starts_ready, 1)
            for m in (0, 2, 4, 6):
                dve.wait_ge(xs_done, m + 1)
                ts_op(XS[:, m, 0:SLOTS], psum[:, m % 4, :], v_("norm2", m), None, MUL).then_inc(xs_dve, 1)

            dve.wait_ge(ct_done, 1)
            for s in range(0, SB, 2):
                last = V_.tensor_copy(CT[:, s:s + 2, :], proj_bank(6 + s // 2))
            last.then_inc(ct_sb, 1)

            cnt_j = CNT.unsqueeze(2).to_broadcast([P, EXPERTS, MORE])
            start_j = START.unsqueeze(2).to_broadcast([P, EXPERTS, MORE])
            pass_of = c_("pass_of").rearrange("p (e c) -> p e c", e=EXPERTS)

            def by_pass(v):
                return v.rearrange("p (e c) -> p e c", e=EXPERTS)

            step.mark(tt_op(by_pass(MF), cnt_j, pass_of, GT))
            step.mark(V_.memset(onesrow, 1.0))
            step(ts_op(by_pass(MS), cnt_j, -float(CH), None, ADD))
            step(tt_op(by_pass(MS), by_pass(MS), pass_of, MIN))
            step(tt_op(by_pass(MS), by_pass(MS), start_j, ADD))
            step(V_.tensor_tensor_scan(MC, onesrow, MF, 0.0, MUL, ADD))
            step(tt_op(MB, MC, MF, SUB))
            shape = [P, TASKS, NJ]
            step(tt_op(TOH, MB.unsqueeze(1).to_broadcast(shape), iota[:, 0:TASKS].unsqueeze(2).to_broadcast(shape), EQ))
            step(tt_op(TOH, TOH, MF.unsqueeze(1).to_broadcast(shape), MUL))
            units_of = c_("units_of").rearrange("p (k j) -> p k j", k=3)
            for k in range(4):
                v = MS if k == 3 else units_of[:, k, :]
                step(tt_op(TMUL, TOH, v.unsqueeze(1).to_broadcast(shape), MUL))
                step(V_.tensor_reduce(TASK[:, k, :], TMUL, AX.X, ADD))
            step.mark(V_.tensor_copy(taski[:, 0:4 * TASKS], TASK.rearrange("p a b -> p (a b)")))
            step.sync()
            V_.tensor_copy(taski[:, 4 * TASKS:4 * TASKS + 1], MC[:, NJ - 1:NJ]).then_inc(tasks_ready, 1)

            def activations(par):
                return tt_op(AT[0:CH, par], SL[0:CH, par], psum[0:CH, par, D_EXP:2 * D_EXP], MUL)

            def turned(par):
                return V_.tensor_copy(AE[:, par], psum[:, 4 + par, 0:2 * CH].rearrange("p (f n) -> p f n", f=2))

            def results(par):
                b = (2, 6)[par]
                return V_.tensor_copy(YO[0:CH, par, :], psum[0:CH, b:b + 2, :].rearrange("p a b -> p (a b)"))

            def experts(e, i=0):
                dve.wait_ge(at_tr, i * 2 + (e + 1))
                turned(e % 2).then_inc(ae_ready, 1)
                if e < EXPERTS - 1:
                    dve.wait_ge(silu_done, i * 2 + (e + 2))
                    activations((e + 1) % 2).then_inc(at_ready, 1)
                dve.wait_ge(unit_used, i * 6 + (U_EXP + 5 + 3 * e) if e < EXPERTS - 1 else UNITS)
                if e >= 2:
                    dve.wait_ge(y_stored, i * 32 + 16 * (e - 1))
                results(e % 2).then_inc(y_copied, 1)

            dve.wait_ge(silu_done, 1)
            activations(0).then_inc(at_ready, 1)
            experts(0)
            experts(1)
            with dve.Fori(0, (EXPERTS - 4) // 2) as i:
                experts(2, i)
                experts(3, i)
            experts(EXPERTS - 2)
            experts(EXPERTS - 1)

            dve.wait_ge(tasks_ready, 1)
            total = dve.value_load(taski[0:1, 4 * TASKS:4 * TASKS + 1], min_val=0, max_val=TASKS)
            with dve.If(total > 0):
                dve.wait_ge(y_stored, 16 * (EXPERTS - 1))
                with dve.Fori(0, total) as t:
                    dve.wait_ge(more_silu, t + 1)
                    activations(0).then_inc(more_at, 1)
                    dve.wait_ge(more_tr, t + 1)
                    turned(0).then_inc(more_ae, 1)
                    dve.wait_ge(unit_used, t + (UNITS + 1))
                    results(0).then_inc(more_copied, 1)
                    dve.wait_ge(more_stored, t * 16 + 16)
                dve.nop()
            dve.nop()
            dve.wait_ge(y_done, 1)
            for tt in range(TT):
                last = tt_op(X[:, tt, :], X[:, tt, :], psum[:, 2 * tt:2 * tt + 2, :].rearrange("p a b -> p (a b)"), ADD)
            last.then_inc(final_x, 1)
            mean_squares(9, [(0, 2, D)])
            dve.wait_ge(final_x, 1)
            for tt in range(TT):
                stt(HN[:, tt, :], X[:, tt, :], rstd[:, 9, tt:tt + 1], r_("final"), MUL, MUL).then_inc(out_ready, 1)


def constants():
    c = np.zeros((P, CC.size), np.float32)
    i, j = np.arange(P)[:, None], np.arange(P)[None, :]
    c[:, CC["ident"]] = i == j
    c[:, CC["tri"]] = i <= j
    c[:, CC["ones"]] = 1
    c[:, CC["stri"]] = i < j
    c[:, CC["btri"]] = (i <= j) & (i // GLA_CHUNK == j // GLA_CHUNK)
    q = np.arange(P)[:, None]
    c[:, CC["causal"]] = np.where(np.concatenate([j <= q, np.arange(S)[None] <= q + P], 1), 0, np.float32(NEG))
    c[:, CC["iota"]] = np.arange(SLOTS)
    inv = np.float32(10000.0) ** (-(np.arange(HALF, dtype=np.float32) * np.float32(2.0) / np.float32(ROPE)))
    ang = np.arange(S, dtype=np.float32)[:, None] * inv[None, :].astype(np.float32)
    for name, f in (("cos", np.cos), ("sin", np.sin)):
        c[:, CC[name]] = f(ang).astype(np.float32).reshape(TT, P, HALF).transpose(1, 0, 2).reshape(P, -1)
    pos = np.arange(PAD) + 1
    c[:, CC["rcount"]] = np.concatenate([1.0 / np.minimum(pos, w) for w in POOL_WINDOWS])
    dist = 2 * WINDOW - 1 - np.arange(P + S)
    d = np.maximum(dist, 1).astype(np.float32)
    exact = BUCKETS // 2
    large = exact + (np.log(d / exact) / np.float32(math.log(MAX_DIST / exact)) * (BUCKETS - exact)).astype(np.int32)
    bucket = np.where(dist < exact, dist, np.minimum(large, BUCKETS - 1))
    valid = (dist >= 0) & (dist < WINDOW)
    c[0:BUCKETS, CC["bucket"]] = (bucket[None] == np.arange(BUCKETS)[:, None]) & valid[None]
    c[0:SWA_HEADS, CC["line"]] = np.where(valid, 0, np.float32(NEG))
    for h in range(FOX_HEADS):
        c[h, CC["foxk"].start + h * S:CC["foxk"].start + (h + 1) * S] = HD ** 0.5
        c[h, CC["foxq"].start + h * P:CC["foxq"].start + (h + 1) * P] = -HD ** 0.5
    e = np.arange(EXPERTS)
    gate = np.where(e == 0, U_EXP, U_EXP - 1 + 3 * e)
    down = np.where(e == EXPERTS - 1, UNITS - 1, U_EXP + 4 + 3 * e)
    c[:, CC["units_of"]] = np.repeat(np.stack([gate, gate + 1, down]), MORE, axis=1).reshape(-1)
    c[:, CC["pass_of"]] = np.tile(CH * (1 + np.arange(MORE)), EXPERTS)
    return c


def by_columns(w, width=FF_CHUNK):
    K, N = w.shape
    return w.reshape(K // P, P, N // width, width).transpose(2, 1, 0, 3).reshape(N // width, P, UNIT)


def by_rows(w):
    K, N = w.shape
    return w.reshape(K // (2 * P), 2, P, N).transpose(0, 2, 1, 3).reshape(K // (2 * P), P, UNIT)


def interleaved(gate, up, down):
    order = [gate[0], up[0]]
    for n in range(len(gate) - 1):
        order += [gate[n + 1], up[n + 1], down[n]]
    return order + [down[-1]]


def kernel(**inputs):
    import concourse.bacc as bacc
    from concourse.bass_utils import run_bass_kernel_spmd

    a = {k: np.asarray(v) for k, v in inputs.items()}
    one = {k: v[0] for k, v in a.items() if k not in ("rel_bias", "norm_f_g_2")}

    w = one["w_in"]
    swa, fox = (SWA_HEADS + 2 * SWA_KV) * HD, 3 * FOX_HEADS * HD + FOX_HEADS
    heads = [w[:, h * HD:(h + 1) * HD] for h in range(SWA_HEADS)]
    qa = [heads[4 * k + j] for j in range(4) for k in range(2)]
    ka_va = w[:, SWA_HEADS * HD:swa]
    f = w[:, swa:swa + fox]
    m = w[:, swa + fox:]
    F = FOX_HEADS * HD
    tail = np.concatenate([m[:, Q_RANK:], f[:, 3 * F:], np.zeros((D, FF_CHUNK - KV_RANK - ROPE - FOX_HEADS), np.float32)], 1)
    cols = np.concatenate([m[:, :Q_RANK], tail, f[:, 2 * F:3 * F], ka_va, *qa, f[:, :F], f[:, F:2 * F]], 1)
    units = list(by_columns(cols)) + list(by_rows(one["w_out"]))
    up = by_columns(one["w_up"])
    units += interleaved(up[:FF_CHUNKS], up[FF_CHUNKS:], by_rows(one["w_down"]))
    w = one["w_in_2"]
    widths = (GLA_KEY, GLA_KEY, GLA_VAL, GLA_VAL, GLA_RANK, POOL_G * P, D, D)
    q, k, v, r, low, pool, gg, gp = np.split(w, np.cumsum(widths)[:-1], axis=1)
    units += list(by_columns(np.concatenate([q, k, v, pool, r, gg, gp], 1)))
    branch = [one["w_gla_branch_2"], one["w_pool_branch_2"]]
    packed = [b.reshape(4, P, 2, 512).transpose(2, 1, 0, 3).reshape(2, P, UNIT) for b in branch]
    units += [packed[n][j] for j in range(2) for n in range(2)]
    units += list(by_rows(one["w_out_2"]))
    eg, eu, ed = one["w_exp_gate_2"], one["w_exp_up_2"], one["w_exp_down_2"]
    units += interleaved([by_columns(x)[0] for x in eg], [by_columns(x)[0] for x in eu], [by_rows(x)[0] for x in ed])
    units = np.stack(units)
    assert units.shape == (UNITS, P, UNIT)

    vec = np.zeros((P, VC.size), np.float32)
    for name, src in (("attn_pre", "attn_pre_norm"), ("group", "group_norm"), ("ffn_pre", "ffn_pre_norm"),
                      ("norm1", "norm1_g_2"), ("norm2", "norm2_g_2"), ("q_lat", "q_latent_norm"),
                      ("kv_lat", "kv_latent_norm"), ("pool_scale", "pool_scale_2"), ("gla", "gla_norm_g_2"),
                      ("conv", "conv_w"), ("conv_b", "conv_b")):
        vec[:, VC[name]] = one[src].reshape(-1, P).T
    rows = np.zeros((1, RC.size), np.float32)
    router_b = np.concatenate([one["b_router_group_2"], one["b_router_expert_2"].reshape(-1)])
    for name, value in (("attn_post", one["attn_post_norm"]), ("ffn_post", one["ffn_post_norm"]),
                        ("final", a["norm_f_g_2"]), ("b_alpha", one["b_alpha_2"]), ("router_b", router_b),
                        ("forget", one["forget_bias"]), ("sinks", one["swa_sinks"])):
        rows[0, RC[name]] = value
    small = np.zeros((P, SC.size), np.float32)

    def by_k(w):
        return w.reshape(-1, P, w.shape[1]).transpose(1, 0, 2).reshape(P, -1)

    small[:, SC["uq"]] = by_k(one["w_uq"])
    small[:, SC["ukv"]] = one["w_ukv"]
    small[0:GLA_RANK, SC["w_alpha"]] = one["w_alpha_up_2"]
    small[:, SC["a_low"]] = by_k(low)
    router = np.concatenate([one["w_router_group_2"], one["w_router_expert_2"].transpose(1, 0, 2).reshape(D, EXPERTS)], 1)
    small[:, SC["router"]] = by_k(router)
    small[:, SC["pool_w"]] = one["pool_w_2"].transpose(1, 0, 2).reshape(P, -1)
    small[0:BUCKETS, SC["rel"]] = a["rel_bias"]

    x = np.ascontiguousarray(a["x"][0].reshape(TT, P, D).transpose(1, 0, 2))
    nc = bacc.Bacc("TRN2", target_bir_lowering=False, num_devices=1)
    arrays = {"x_in": x, "units_in": units, "const_in": constants(), "vec_in": vec, "rows_in": rows, "small_in": small}
    args = [nc.dram_tensor(k, v.shape, mybir.dt.float32, kind="ExternalInput").ap() for k, v in arrays.items()]
    out = nc.dram_tensor("out", [TT, P, D], mybir.dt.float32, kind="ExternalOutput").ap()
    build(nc, *args, out)
    r = run_bass_kernel_spmd(nc, [arrays], core_ids=[0])
    return r.results[0]["out"].reshape(1, S, D)
```

```python
import math
from contextlib import ExitStack

import numpy as np

import concourse.bass as bass
from concourse import mybir
from concourse.alu_op_type import AluOpType as ALU

P = 128
S = 256
TT = S // P
D = 1024
KD = D // P
HD = 64
SWA_HEADS, SWA_KV, FOX_HEADS, MLA_HEADS = 8, 2, 4, 4
HEADS = SWA_HEADS + FOX_HEADS + MLA_HEADS
WINDOW = 128
NOPE, ROPE = 64, 32
HALF = ROPE // 2
MLA_QK = NOPE + ROPE
Q_RANK, KV_RANK = 256, 128
BUCKETS, MAX_DIST = 32, 128
D_FF = 2816
FF_CHUNK = 256
FF_CHUNKS = D_FF // FF_CHUNK
FF_TILES = D_FF // P
EPS = 1e-6
NEG = -1e30
GLA_HEADS, GLA_DK, GLA_DV, GLA_RANK, GLA_CHUNK = 4, 64, 128, 16, 64
GLA_KEY, GLA_VAL = GLA_HEADS * GLA_DK, GLA_HEADS * GLA_DV
GATE_NORMALIZER = 16.0
POOL_WINDOWS = (2, 4, 8, 16)
POOL_G = len(POOL_WINDOWS)
PAD = max(POOL_WINDOWS)
GROUPS, PER_GROUP = 4, 8
EXPERTS = GROUPS * PER_GROUP
TOP_K = 2
SLOTS = S * TOP_K
SB = SLOTS // P
CH = 64
MORE = S // CH - 1
TASKS = SLOTS // CH
D_EXP = 256

RING = 6
UNIT = 2048
U_PROJ = 0
U_WOUT = U_PROJ + 8
U_FFN = U_WOUT + 4
U_GLA = U_FFN + 3 * FF_CHUNKS
U_BRANCH = U_GLA + 16
U_WOUT2 = U_BRANCH + 4
U_EXP = U_WOUT2 + 4
UNITS = U_EXP + 3 * EXPERTS


class Columns:

    def __init__(self):
        self.at, self.size = {}, 0

    def add(self, name, n):
        self.at[name] = (self.size, self.size + n)
        self.size += n

    def __getitem__(self, name):
        a, b = self.at[name]
        return slice(a, b)


CC = Columns()
for _n, _w in (("ident", P), ("tri", P), ("ones", P), ("stri", P), ("btri", P), ("causal", P + S),
               ("iota", SLOTS), ("cos", TT * HALF), ("sin", TT * HALF), ("rcount", POOL_G * PAD),
               ("bucket", P + S), ("line", P + S), ("foxq", FOX_HEADS * P), ("foxk", FOX_HEADS * S),
               ("units_of", 3 * EXPERTS * MORE), ("pass_of", EXPERTS * MORE)):
    CC.add(_n, _w)
VC = Columns()
for _n, _w in (("attn_pre", KD), ("group", KD), ("ffn_pre", KD), ("norm1", KD), ("norm2", KD),
               ("q_lat", Q_RANK // P), ("kv_lat", 1), ("pool_scale", POOL_G), ("gla", GLA_HEADS),
               ("conv", 3 * 2 * FF_TILES), ("conv_b", 2 * FF_TILES)):
    VC.add(_n, _w)
RC = Columns()
for _n, _w in (("attn_post", D), ("ffn_post", D), ("final", D), ("b_alpha", GLA_KEY),
               ("router_b", GROUPS + EXPERTS), ("forget", FOX_HEADS), ("sinks", SWA_HEADS)):
    RC.add(_n, _w)
SC = Columns()
for _n, _w in (("uq", 2 * MLA_HEADS * MLA_QK), ("ukv", MLA_HEADS * (NOPE + HD)), ("w_alpha", GLA_KEY),
               ("a_low", KD * GLA_RANK), ("router", KD * (GROUPS + EXPERTS)), ("pool_w", POOL_G * P),
               ("rel", SWA_HEADS)):
    SC.add(_n, _w)


class Chain:

    def __init__(self, engine, sem):
        self.engine, self.sem, self.n, self.extra = engine, sem, 0, 0

    def mark(self, instruction):
        instruction.then_inc(self.sem, 1)
        self.n += 1

    def sync(self):
        self.engine.wait_ge(self.sem, self.n + self.extra)

    def __call__(self, instruction):
        self.mark(instruction)
        self.sync()


def build(nc, x_in, units_in, const_in, vec_in, rows_in, small_in, out):
    fp32, i32, f32r = mybir.dt.float32, mybir.dt.int32, mybir.dt.float32r
    ACT = mybir.ActivationFunctionType
    AX = mybir.AxisListType
    MUL, ADD, SUB, MAX, MIN, EQ, GT = ALU.mult, ALU.add, ALU.subtract, ALU.max, ALU.min, ALU.is_equal, ALU.is_gt
    ds = bass.ds
    mm = nc.tensor.matmul

    results_dram = nc.dram_tensor("results_scratch", [SLOTS + CH, D], fp32, kind="Internal").ap()
    line_dram = nc.dram_tensor("line_scratch", [SWA_HEADS, P, P + S], fp32, kind="Internal").ap()

    ctx = ExitStack()
    with ctx:
        def sb(name, shape, dt=fp32):
            return ctx.enter_context(nc.sbuf_tensor(name, shape, dt))

        def sem(name):
            return ctx.enter_context(nc.semaphore(name))

        ring = sb("ring", [P, RING, UNIT])
        const = sb("const", [P, CC.size])
        vec = sb("vec", [P, VC.size])
        with nc.sbuf_tensor("rows", [P, RC.size], fp32) as rows:
            pass
        third_low = sb("third_low", [P, UNIT], f32r)
        sb("rows_kept", [P, RC.size - UNIT])
        assert RC["ffn_post"].stop == UNIT
        small = sb("small", [P, SC.size])
        X = sb("X", [P, TT, D])
        with nc.sbuf_tensor("HN", [P, TT, D], fp32) as HN:
            pass
        third_high = sb("third_high", [P, UNIT], f32r)
        with nc.sbuf_tensor("HT", [P, KD, S], fp32) as HT:
            pass
        XWH, XWL = (sb(f"xw_{part}", [P, 2, KD, CH], f32r) for part in ("high", "low"))
        junk = sb("junk", [P, D])
        ss = sb("ss", [P, 11, 8])
        ms = sb("ms", [P, 11, 8])
        rstd = sb("rstd", [P, 11, 8])
        neghalf = sb("neghalf", [P, 8])
        ARENA = 22600
        FFN_FLOAT32, EXPERTS_FLOAT32 = 6144, 13672
        starti = sb("starti", [P, EXPERTS], i32)
        taski = sb("taski", [P, 4 * TASKS + 1], i32)
        psum = ctx.enter_context(nc.psum_tensor("psum", [P, 8, 512], fp32))
        with nc.sbuf_tensor("arena", [P, ARENA], fp32) as arena:
            pass
        with ExitStack() as space:
            def parts_tensor(name, shape):
                return [space.enter_context(nc.sbuf_tensor(f"{name}_{part}", [P, *shape], f32r))
                        for part in ("high", "low")]

            space.enter_context(nc.sbuf_tensor("ffn_float32", [P, FFN_FLOAT32], fp32))
            HTH, HTL = parts_tensor("ht", (KD, S))
            AFH, AFL = parts_tensor("af", (2, 2, S))
            FWH, FWL = parts_tensor("ffn_w", (2, UNIT))
        with ExitStack() as space:
            space.enter_context(nc.sbuf_tensor("experts_float32", [P, EXPERTS_FLOAT32], fp32))
            AEH, AEL = parts_tensor("ae", (2, 2, CH))
            EWH, EWL = parts_tensor("expert_w", (2, UNIT))

        class Arena:

            def __init__(self):
                self.at = 0

            def tile(self, *dims):
                n = math.prod(dims)
                v = arena[:, self.at:self.at + n]
                self.at += n
                assert self.at <= ARENA, self.at
                if len(dims) == 1:
                    return v
                names = "abcd"[:len(dims)]
                return v.rearrange(f"p ({' '.join(names)}) -> p {' '.join(names)}",
                                   **{k: d for k, d in zip(names[1:], dims[1:])})

        def c_(name):
            return const[:, CC[name]]

        def v_(name, i):
            a = VC[name].start + i
            return vec[:, a:a + 1]

        def r_(name):
            return rows[:, RC[name]]

        def s_(name):
            return small[:, SC[name]]

        ident, ones, tri, stri, btri = c_("ident"), c_("ones"), c_("tri"), c_("stri"), c_("btri")
        causal, iota = c_("causal"), c_("iota")

        A = Arena()
        bias = A.tile(SWA_HEADS, P + S)
        line = A.tile(P + S)
        QA, KA, VA = A.tile(4, S), A.tile(S), A.tile(TT, P)
        QF, KF, VF = A.tile(2, S), A.tile(2, S), A.tile(TT, 256)
        CQ, CK = A.tile(TT, Q_RANK), A.tile(TT, 164)
        CQT, CKT = A.tile(2, S), A.tile(S)
        QM, KM = A.tile(TT, MLA_HEADS, MLA_QK), A.tile(TT, MLA_HEADS, MLA_QK)
        VM = A.tile(TT, MLA_HEADS, HD)
        QMT, KMT = A.tile(MLA_HEADS, S), A.tile(MLA_HEADS, S)
        QR = A.tile(TT, MLA_HEADS + 1, ROPE)
        rot = A.tile(4, TT, (MLA_HEADS + 1) * HALF)
        FT = A.tile(S)
        fz, fabs, fexp, flog, flf = (A.tile(TT, FOX_HEADS) for _ in range(5))
        NS = 3
        SM = A.tile(NS, P + S + 2)
        PT = A.tile(2, 3, P)
        O = A.tile(TT, D)
        nmax, psums, rsum = A.tile(HEADS, 2), A.tile(HEADS, 2), A.tile(HEADS, 2)
        A = Arena()
        U = A.tile(2, 4, S)
        G = A.tile(2, 2, S)
        AF = A.tile(2, 2, S)
        T2 = A.tile(TT, D)
        assert A.at <= FFN_FLOAT32
        A = Arena()
        AL = A.tile(S)
        SP = arena[:, A.at:A.at + KD * S].rearrange("p (a b) -> p a b", a=KD)
        z2, zabs, zexp, LA = A.tile(TT, GLA_KEY), A.tile(TT, GLA_KEY), A.tile(TT, GLA_KEY), A.tile(TT, GLA_KEY)
        BC, EB, ENB, KE = A.tile(2, S), A.tile(2, S), A.tile(2, S), A.tile(2, S)
        DEC = A.tile(2, 4)
        QD, KDE, KEND = A.tile(2, S), A.tile(2, S), A.tile(2, S)
        QZ = A.tile(2, TT, 2, P)
        KET, V = A.tile(TT, GLA_KEY), A.tile(TT, GLA_VAL)
        ST = A.tile(TT, GLA_HEADS, P)
        SS = A.tile(3, 2, S)
        OHN, OT = A.tile(TT, GLA_VAL), A.tile(4, S)
        UP, PA, PB = A.tile(POOL_G, PAD + S), A.tile(POOL_G, PAD + S), A.tile(POOL_G, PAD + S)
        PM, YP, RS = A.tile(POOL_G, S), A.tile(POOL_G, S), A.tile(4, S)
        SG = A.tile(KD, S)
        T1a, T1b = A.tile(2, S), A.tile(2, S)
        A = Arena()
        NR = GROUPS + EXPERTS
        LG = A.tile(TT, NR)
        EM, EQX, CAND, OH1, OH2, M, RK, PR = (A.tile(TT, EXPERTS) for _ in range(8))
        g4a, g4b, g4c, g4d = (A.tile(TT, GROUPS) for _ in range(4))
        col = A.tile(16, TT)
        CNT, CUM, START = A.tile(EXPERTS), A.tile(EXPERTS), A.tile(EXPERTS)
        NJ = EXPERTS * MORE
        MF, MC, MS, MB, onesrow = (A.tile(NJ) for _ in range(5))
        TASK = A.tile(4, TASKS)
        PG, WP, WQ = A.tile(TT, SLOTS), A.tile(TT, SLOTS), A.tile(TT, SLOTS)
        TOH, TMUL = (v.rearrange("p a b -> p (a b)")[:, 0:TASKS * NJ].rearrange("p (a b) -> p a b", a=TASKS)
                     for v in (PG, WP))
        CT = A.tile(SB, S)
        XS = A.tile(KD, SLOTS + CH)
        SL, AT = A.tile(2, D_EXP), A.tile(2, D_EXP)
        XW, AE = A.tile(KD, CH), A.tile(2, CH)
        YO = A.tile(2, D)
        YS = XS.rearrange("p a b -> p (a b)")[:, 0:SB * D].rearrange("p (a b) -> p a b", a=SB)
        assert A.at <= EXPERTS_FLOAT32, A.at

        x_loaded, const_loaded, vec_loaded, rows_loaded, small_loaded = map(
            sem, ("x_loaded", "const_loaded", "vec_loaded", "rows_loaded", "small_loaded"))
        ident_loaded = sem("ident_loaded")
        unit_loaded = [sem(f"unit_loaded{i}") for i in range(RING)]
        unit_used = sem("unit_used")
        squares_summed, ms_ready, rstd_ready = map(sem, ("squares_summed", "ms_ready", "rstd_ready"))
        hn_dve, hn_act, tr_done, ht_dve, ht_act = map(sem, ("hn_dve", "hn_act", "tr_done", "ht_dve", "ht_act"))
        x_ready, y_done, t2_ready = sem("x_ready"), sem("y_done"), sem("t2_ready")
        line_done, line_sb, line_stored, bias_loaded = map(
            sem, ("line_done", "line_sb", "line_stored", "bias_loaded"))
        evac_dve, evac_act = sem("evac_dve"), sem("evac_act")
        lat_hn, lat_tr, lat_ct, lat_up, q_split, qk_rot, qk_tr, qmt_sb, kmt_sb = map(
            sem, ("lat_hn", "lat_tr", "lat_ct", "lat_up", "q_split", "qk_rot", "qk_tr", "qmt_sb", "kmt_sb"))
        fz_ready, flog_ready, flf_ready, ft_done, ft_sb = map(
            sem, ("fz_ready", "flog_ready", "flf_ready", "ft_done", "ft_sb"))
        s_done, s_read, mx_ready, exp_done, pt_done, pt_sb, pv_done, o_sb = map(
            sem, ("s_done", "s_read", "mx_ready", "exp_done", "pt_done", "pt_sb", "pv_done", "o_sb"))
        hi_ready, lo_ready, ht_hi, ht_lo, af_parts = map(sem, ("hi_ready", "lo_ready", "ht_hi", "ht_lo", "af_parts"))
        tap_last, gate_conv, gelu_done, act_ready = map(
            sem, ("tap_last", "gate_conv", "gelu_done", "act_ready"))
        al_done, al_sb, z_done, z_abs, z_log, la_ready, bc_done, bc_sb, exps_done = map(
            sem, ("al_done", "al_sb", "z_done", "z_abs", "z_log", "la_ready", "bc_done", "bc_sb", "exps_done"))
        g_dve, g_act, kend_tr, kend_sb, v_sb, st_done, st_sb, inc_done, states_ready, o_done, ohn_ready = map(
            sem, ("g_dve", "g_act", "kend_tr", "kend_sb", "v_sb", "st_done", "st_sb", "inc_done",
                  "states_ready", "o_done", "ohn_ready"))
        ot_tr, ot_sb, pool_in, pool_sums, pm_ready, pool_done, yp_sb, merged = map(
            sem, ("ot_tr", "ot_sb", "pool_in", "pool_sums", "pm_ready", "pool_done", "yp_sb", "merged"))
        lg_done, top_in, top_exp, top_e, top_eexp, m_ready, rank_done, pg_ready, wp_ready = map(
            sem, ("lg_done", "top_in", "top_exp", "top_e", "top_eexp", "m_ready", "rank_done", "pg_ready",
                  "wp_ready"))
        tasks_ready, results_in_dram = sem("tasks_ready"), sem("results_in_dram")
        xs_done, xs_dve, xs_act, ct_done, ct_sb = map(sem, ("xs_done", "xs_dve", "xs_act", "ct_done", "ct_sb"))
        pad_zero, starts_ready, xw_hi, xw_lo, silu_done, at_ready, at_tr, ae_hi, ae_lo, y_copied, y_stored = map(
            sem, ("pad_zero", "starts_ready", "xw_hi", "xw_lo", "silu_done", "at_ready", "at_tr", "ae_hi", "ae_lo",
                  "y_copied", "y_stored"))
        more_loaded, more_xw, more_up, more_silu, more_at, more_tr, more_ae, more_copied, more_stored = map(
            sem, ("more_loaded", "more_xw", "more_up", "more_silu", "more_at", "more_tr", "more_ae",
                  "more_copied", "more_stored"))
        ys_loaded = [sem(f"ys_loaded{s}") for s in range(SB)]
        out_ready, out_stored, final_x = sem("out_ready"), sem("out_stored"), sem("final_x")
        up_conv, pool_zero = sem("up_conv"), sem("pool_zero")
        dve_steps, act_steps, pool_steps = sem("dve_steps"), sem("act_steps"), sem("pool_steps")

        block = ctx.enter_context(nc.Block())

        def unit(engine, n, i=0):
            engine.wait_ge(unit_loaded[n % RING], 16 * (n // RING + 1) + 16 * i)
            return ring[:, n % RING, :]

        def splits(n):
            return n - U_FFN + 1 if n < U_GLA else n - U_EXP + 1 + 3 * FF_CHUNKS

        def parts_slot(n):
            if n < U_GLA:
                return FWH[:, n % 2, :], FWL[:, n % 2, :]
            k = (n - U_EXP) % 3
            return (third_high[:, :], third_low[:, :]) if k == 2 else (EWH[:, k, :], EWL[:, k, :])

        def split_hi(act, n, i=0):
            w = unit(act, n, i)
            before = 2 if n < U_GLA else 3
            if n not in range(U_FFN, U_FFN + 2) and n not in range(U_EXP, U_EXP + 3):
                act.wait_ge(unit_used, i * RING + (n - before + 1))
            nc.scalar.activation(parts_slot(n)[0], w, ACT.Copy).then_inc(hi_ready, 1)

        def split_lo(dve, n, i=0):
            dve.wait_ge(hi_ready, i * RING + splits(n))
            h, l = parts_slot(n)
            nc.vector.tensor_tensor(l, ring[:, n % RING, :], h.bitcast(fp32), SUB).then_inc(lo_ready, 1)

        def proj_bank(i):
            return psum[:, i % 8, :].rearrange("p (a b) -> p a b", a=2)

        @block.sync
        def _(sp):
            sp.dma_start(X[:, :, :], x_in).then_inc(x_loaded, 16)
            sp.dma_start(ident, const_in[:, CC["ident"]]).then_inc(ident_loaded, 16)
            sp.dma_start(vec[:, :], vec_in).then_inc(vec_loaded, 16)
            for n in range(RING):
                sp.dma_start(ring[:, n, :], units_in[n]).then_inc(unit_loaded[n], 16)
                if n == 1:
                    sp.dma_start(const[:, P:], const_in[:, P:]).then_inc(const_loaded, 16)
                    sp.dma_start(small[:, :], small_in).then_inc(small_loaded, 16)
                if n == 3:
                    sp.dma_start(rows[:, :], rows_in.to_broadcast([P, RC.size])).then_inc(rows_loaded, 16)
            rounds = (UNITS - RING) // RING
            with sp.Fori(0, rounds) as i:
                for k in range(RING):
                    sp.wait_ge(unit_used, i * RING + (k + 1))
                    sp.dma_start(ring[:, k, :], units_in[ds(i * RING + (RING + k), 1)]
                                 .rearrange("a p n -> p (a n)")).then_inc(unit_loaded[k], 16)
            for n in range(RING + rounds * RING, UNITS):
                sp.wait_ge(unit_used, n - RING + 1)
                sp.dma_start(ring[:, n % RING, :], units_in[n]).then_inc(unit_loaded[n % RING], 16)

            sp.wait_ge(tasks_ready, 1)
            total = sp.value_load(taski[0:1, 4 * TASKS:4 * TASKS + 1], min_val=0, max_val=TASKS)
            with sp.If(total > 0):
                with sp.Fori(0, total) as t:
                    sp.wait_ge(unit_used, t + UNITS)
                    for k in range(3):
                        u = sp.value_load(taski[0:1, ds(t + k * TASKS, 1)], min_val=0, max_val=UNITS - 1)
                        sp.dma_start(ring[:, k, :], units_in[ds(u, 1)]
                                     .rearrange("a p n -> p (a n)")).then_inc(more_loaded, 16)
                sp.nop()
            sp.nop()
            sp.wait_ge(results_in_dram, 1)
            for s in range(SB):
                sp.dma_start(YS[:, s, :], results_dram[s * P:(s + 1) * P]).then_inc(ys_loaded[s], 16)
            for tt in range(TT):
                sp.wait_ge(out_ready, tt + 1)
                sp.dma_start(out[tt], HN[:, tt, :]).then_inc(out_stored, 16)
            sp.wait_ge(out_stored, 16 * TT)

        @block.tensor
        def _(pe):
            def transposes(stage):
                pe.wait_ge(hn_dve, stage + 1)
                pe.wait_ge(hn_act, stage + 1)
                for b in range(KD // 2):
                    for k in range(2):
                        for tt in range(TT):
                            at = k * S + tt * P
                            last = nc.tensor.transpose(psum[:, b, at:at + P],
                                                       HN[:, tt, (2 * b + k) * P:(2 * b + k + 1) * P], ident)
                    last.then_inc(tr_done, 1)

            def ht_ready(stage):
                pe.wait_ge(ht_dve, stage + (stage < 2))
                pe.wait_ge(ht_act, stage + (stage < 2))

            def features(bank, w, half, stride=FF_CHUNK):
                for k in range(KD):
                    last = mm(psum[:, bank, half * S:half * S + S], w[:, k * stride + half * P:k * stride + half * P + P],
                              HT[:, k, :], start=k == 0, stop=k == KD - 1)
                return last

            def tokens(bank, w, a, n, at):
                for tt in range(TT):
                    for k in range(KD):
                        last = mm(psum[:, bank, tt * S + at:tt * S + at + n] if n != P else
                                  psum[:, bank, at + tt * P:at + tt * P + n],
                                  HT[:, k, tt * P:(tt + 1) * P], w[:, k * FF_CHUNK + a:k * FF_CHUNK + a + n],
                                  start=k == 0, stop=k == KD - 1)
                return last

            def rows_out(n0, count, lhs, ready=None):
                for j in range(count):
                    if ready is not None:
                        pe.wait_ge(ready, max(j + 1, 2))
                    w = unit(pe, n0 + j)
                    for kk in range(2):
                        for tt in range(TT):
                            for n in range(2):
                                last = mm(psum[:, 4 + 2 * tt + n, :], lhs[:, 2 * j + kk, tt * P:(tt + 1) * P],
                                          w[:, kk * D + n * 512:kk * D + n * 512 + 512],
                                          start=j == 0 and kk == 0, stop=j == count - 1 and kk == 1)
                    last.then_inc(unit_used, 1)

            pe.wait_ge(ident_loaded, 16)
            transposes(0)
            ht_ready(0)
            for i in range(8):
                if i == 3:
                    pe.wait_ge(const_loaded, 16)
                    pe.wait_ge(small_loaded, 16)
                    mm(psum[0:SWA_HEADS, 4, 0:P + S], s_("rel")[0:BUCKETS, :], c_("bucket")[0:BUCKETS, :],
                       start=True, stop=True).then_inc(line_done, 1)
                if i == 4:
                    pe.wait_ge(line_sb, 1)
                w = unit(pe, U_PROJ + i)
                if i == 0:
                    last = tokens(0, w, 0, 256, 0)
                elif i == 1:
                    last = tokens(1, w, 0, 164, 0)
                elif i == 2:
                    last = tokens(2, w, 0, 256, 0)
                elif i == 3:
                    features(3, w, 0)
                    last = tokens(3, w, P, P, S)
                else:
                    features(i, w, 0)
                    last = features(i, w, 1)
                last.then_inc(unit_used, 1)

            pe.wait_ge(lat_hn, 1)
            for tt in range(TT):
                for k in range(2):
                    nc.tensor.transpose(psum[:, 0, k * S + tt * P:k * S + tt * P + P], CQ[:, tt, k * P:(k + 1) * P],
                                        ident)
            for tt in range(TT):
                last = nc.tensor.transpose(psum[:, 1, tt * P:(tt + 1) * P], CK[:, tt, 0:P], ident)
            last.then_inc(lat_tr, 1)
            pe.wait_ge(flf_ready, 1)
            pe.wait_ge(evac_dve, 4)
            mm(psum[0:FOX_HEADS, 6, 0:S], flf[:, 0, :], const[:, CC["tri"].start:CC["ones"].stop],
               start=True, stop=False)
            mm(psum[0:FOX_HEADS, 6, P:S], flf[:, 1, :], tri, start=False, stop=True).then_inc(ft_done, 1)
            pe.wait_ge(lat_ct, 1)
            pe.wait_ge(evac_act, 4)
            uq = s_("uq").rearrange("p (k n) -> p k n", k=2)
            for tt in range(TT):
                for k in range(2):
                    mm(psum[:, 2 + tt, 0:MLA_HEADS * MLA_QK], CQT[:, k, tt * P:(tt + 1) * P], uq[:, k, :],
                       start=k == 0, stop=k == 1)
                last = mm(psum[:, 4 + tt, :], CKT[:, tt * P:(tt + 1) * P], s_("ukv"), start=True, stop=True)
            last.then_inc(lat_up, 1)
            pe.wait_ge(qk_rot, 1)
            for tt in range(TT):
                for h in range(MLA_HEADS):
                    nc.tensor.transpose(psum[0:MLA_QK, tt, h * P:(h + 1) * P], QM[:, tt, h, :], ident)
                    last = nc.tensor.transpose(psum[0:MLA_QK, 2 + tt, h * P:(h + 1) * P], KM[:, tt, h, :], ident)
            last.then_inc(qk_tr, 1)
            pe.wait_ge(ft_sb, 1)
            pe.wait_ge(qmt_sb, 1)
            pe.wait_ge(kmt_sb, 1)

            def logits(h):
                if h >= 2:
                    pe.wait_ge(s_read, h - 1)
                for qb in range(TT):
                    o = psum[:, 4 + h % 2, 0:P] if qb == 0 else psum[:, 4 + h % 2, P:P + S]
                    nk = P * (qb + 1)
                    q_at = slice(qb * P, (qb + 1) * P)
                    if h < SWA_HEADS:
                        kv, base = h // 4, HD * (h // 4)
                        last = mm(o, QA[base:base + HD, h % 4, q_at], KA[base:base + HD, 0:nk], start=True, stop=True)
                    elif h < SWA_HEADS + FOX_HEADS:
                        f = h - SWA_HEADS
                        base = HD * (f % 2)
                        mm(o, QF[base:base + HD, f // 2, q_at], KF[base:base + HD, f // 2, 0:nk],
                           start=True, stop=False)
                        mm(o, FT[0:FOX_HEADS, q_at], c_("foxk")[0:FOX_HEADS, f * S:f * S + nk],
                           start=False, stop=False)
                        last = mm(o, c_("foxq")[0:FOX_HEADS, f * P:(f + 1) * P], FT[0:FOX_HEADS, 0:nk],
                                  start=False, stop=True)
                    else:
                        m = h - SWA_HEADS - FOX_HEADS
                        last = mm(o, QMT[0:MLA_QK, m, q_at], KMT[0:MLA_QK, m, 0:nk], start=True, stop=True)
                last.then_inc(s_done, 1)

            def value_tile(h, tt):
                if h < SWA_HEADS:
                    return VA[:, tt, HD * (h // 4):HD * (h // 4) + HD]
                if h < SWA_HEADS + FOX_HEADS:
                    return VF[:, tt, HD * (h - SWA_HEADS):HD * (h - SWA_HEADS) + HD]
                return VM[:, tt, h - SWA_HEADS - FOX_HEADS, :]

            logits(0)
            logits(1)
            for h in range(HEADS):
                pe.wait_ge(exp_done, h + 1)
                if h >= 2:
                    pe.wait_ge(pt_sb, h - 1)
                for b in range(3):
                    last = nc.tensor.transpose(psum[:, 6 + h % 2, b * P:(b + 1) * P],
                                               SM[:, h % NS, 1 + b * P:1 + (b + 1) * P], ident)
                last.then_inc(pt_done, 1)
                if h + 2 < HEADS:
                    logits(h + 2)
                pe.wait_ge(pt_sb, h + 1)
                if h % 4 == 0 and h >= 8:
                    pe.wait_ge(o_sb, h // 4 - 1)
                o = psum[:, 2 + (h // 4) % 2, (h % 4) * P:(h % 4 + 1) * P]
                mm(o[:, 0:HD], PT[:, h % 2, 0, :], value_tile(h, 0), start=True, stop=True)
                mm(o[:, HD:P], PT[:, h % 2, 1, :], value_tile(h, 0), start=True, stop=False)
                mm(o[:, HD:P], PT[:, h % 2, 2, :], value_tile(h, 1), start=False, stop=True).then_inc(pv_done, 1)

            transposes(1)
            ht_ready(1)
            rows_out(U_WOUT, 4, HT)

            transposes(2)

            def parts(n, i=0):
                pe.wait_ge(lo_ready, i * RING + splits(n))
                return parts_slot(n)

            def by_parts(o, l, r, start, stop):
                pairs = ((0, 0), (0, 1), (1, 0))[0:2 * len(l) - 1]
                for a, b in pairs:
                    last = mm(o, l[a], r[b], start=start and (a, b) == pairs[0], stop=stop and (a, b) == pairs[-1])
                return last

            def ffn_up(c, n0, i=0, first=False):
                for g in range(2):
                    w = parts(n0 + g, i)
                    for half in range(2):
                        for k in range(KD):
                            if first and g == 0 and half == 0 and k % 2 == 0:
                                pe.wait_ge(ht_lo, k // 2 + 1)
                            a = k * FF_CHUNK + half * P
                            last = by_parts(psum[:, 2 * (c % 2) + g, half * S:half * S + S],
                                            [v[:, a:a + P] for v in w], (HTH[:, k, :], HTL[:, k, :]),
                                            k == 0, k == KD - 1)
                    last.then_inc(unit_used, 1)

            def ffn_down(c, n0, i=0, ready=None, first=False, final=False):
                pe.wait_ge(act_ready, ready)
                w = parts(n0, i)
                for kk in range(2):
                    for tt in range(TT):
                        for n in range(2):
                            a = kk * D + n * 512
                            last = by_parts(psum[:, 4 + 2 * tt + n, :],
                                            [v[:, c % 2, kk, tt * P:(tt + 1) * P] for v in (AFH, AFL)],
                                            [v[:, a:a + 512] for v in w], first and kk == 0, final and kk == 1)
                last.then_inc(unit_used, 1)

            ffn_up(0, U_FFN, first=True)
            for c in range(2):
                ffn_up(c + 1, U_FFN + 2 + 3 * c)
                ffn_down(c, U_FFN + 4 + 3 * c, ready=c + 1, first=c == 0)
            with pe.Fori(0, (FF_CHUNKS - 3) // 2) as i:
                for c in (2, 3):
                    ffn_up(c + 1, U_FFN + 2 + 3 * c, i)
                    ffn_down(c, U_FFN + 4 + 3 * c, i, ready=i * 2 + (c + 1))
            ffn_down(FF_CHUNKS - 1, U_FFN + 3 * FF_CHUNKS - 1, ready=FF_CHUNKS, final=True)

            transposes(3)
            ht_ready(3)
            al = s_("a_low").rearrange("p (k n) -> p k n", k=KD)
            for k in range(KD):
                last = mm(psum[0:GLA_RANK, 4, 0:S], al[:, k, :], HT[:, k, :], start=k == 0, stop=k == KD - 1)
            last.then_inc(al_done, 1)

            def gla_unit(j, bank, major=features):
                w = unit(pe, U_GLA + j)
                if major is tokens:
                    last = tokens(bank, w, 0, 256, 0)
                else:
                    features(bank, w, 0)
                    last = features(bank, w, 1)
                last.then_inc(unit_used, 1)

            gla_unit(0, 0)
            pe.wait_ge(al_sb, 1)
            for tt in range(TT):
                last = mm(psum[:, 5, tt * S:(tt + 1) * S], AL[0:GLA_RANK, tt * P:(tt + 1) * P],
                          s_("w_alpha")[0:GLA_RANK, :], start=True, stop=True)
            last.then_inc(z_done, 1)
            gla_unit(1, 1)
            gla_unit(2, 2, tokens)
            gla_unit(3, 3, tokens)
            pe.wait_ge(la_ready, 1)
            for f in range(2):
                for tt in range(TT):
                    last = mm(psum[:, 4, f * S + tt * P:f * S + (tt + 1) * P], LA[:, tt, f * P:(f + 1) * P], btri,
                              start=True, stop=True)
            last.then_inc(bc_done, 1)
            gla_unit(4, 6)
            gla_unit(5, 7)
            pe.wait_ge(g_dve, 2)
            for tt in range(TT):
                for f in range(2):
                    last = nc.tensor.transpose(psum[:, 0, tt * S + f * P:tt * S + (f + 1) * P],
                                               KEND[:, f, tt * P:(tt + 1) * P], ident)
            last.then_inc(kend_tr, 1)
            for odd in range(2):
                base = HD * odd
                for tt in range(TT):
                    for f in range(2):
                        at = (2 * tt + f) * P
                        last = mm(psum[:, (1, 4)[odd], at:at + P], KDE[base:base + HD, f, tt * P:(tt + 1) * P],
                                  QD[base:base + HD, f, tt * P:(tt + 1) * P], start=True, stop=True)
                last.then_inc(st_done, 1)
            pe.wait_ge(kend_sb, 1)
            pe.wait_ge(v_sb, 2)
            pe.wait_ge(z_abs, 1)
            for n in range(3):
                base = HD * (n % 2)
                b = (2, 3, 5)[n]
                for f in range(2):
                    last = mm(psum[:, b, f * S:(f + 1) * S], KET[base:base + HD, n // 2, f * P:(f + 1) * P],
                              V[base:base + HD, n // 2, f * S:(f + 1) * S], start=True, stop=True)
                last.then_inc(inc_done, 1)
            pe.wait_ge(st_sb, 2)
            pe.wait_ge(states_ready, 3)
            for odd in range(2):
                base = HD * odd
                for tt in range(TT):
                    for f in range(2):
                        h = 2 * f + odd
                        o = psum[:, (1, 4)[odd], (2 * tt + f) * P:(2 * tt + f + 1) * P]
                        chunks = [2 * tt + c for c in range(2) if 2 * tt + c > 0]
                        mm(o, ST[:, tt, h, :], V[:, tt, h * P:(h + 1) * P], start=True, stop=False)
                        for n in chunks:
                            last = mm(o, QZ[base:base + HD, f, tt, n % 2, :],
                                      SS[base:base + HD, n - 1, f, odd * P:(odd + 1) * P],
                                      start=False, stop=n == chunks[-1])
                last.then_inc(o_done, 1)
            pe.wait_ge(pool_in, 2)
            gla_unit(6, 6)
            gla_unit(7, 7)
            for j in range(4):
                gla_unit(8 + j, (2, 3, 0, 5)[j])
            pe.wait_ge(pm_ready, 1)
            pe.wait_ge(g_act, 2)
            pw = s_("pool_w").rearrange("p (g n) -> p g n", g=POOL_G)
            for g in range(POOL_G):
                last = mm(psum[:, 6 + g // 2, (g % 2) * S:(g % 2 + 1) * S], pw[:, g, :], PM[:, g, :],
                          start=True, stop=True)
            last.then_inc(pool_done, 1)
            pe.wait_ge(ohn_ready, 2)
            for k in range(4):
                for tt in range(TT):
                    last = nc.tensor.transpose(psum[:, (1, 4)[k // 2], (k % 2) * S + tt * P:(k % 2) * S + (tt + 1) * P],
                                               OHN[:, tt, k * P:(k + 1) * P], ident)
            last.then_inc(ot_tr, 1)
            pe.wait_ge(g_act, 6)
            for j in range(4):
                gla_unit(12 + j, (2, 3, 0, 5)[j])
            pe.wait_ge(ot_sb, 1)
            pe.wait_ge(yp_sb, 1)
            for j in range(2):
                for src, b0 in ((OT, (6, 2)[j]), (YP, (4, 0)[j])):
                    if j == 0 and src is YP:
                        pe.wait_ge(g_act, 10)
                    w = unit(pe, U_BRANCH + 2 * j + (src is YP))
                    for m in range(4):
                        for k in range(4):
                            last = mm(psum[:, b0 + m // 2, (m % 2) * S:(m % 2 + 1) * S],
                                      w[:, k * 512 + m * P:k * 512 + (m + 1) * P], src[:, k, :],
                                      start=k == 0, stop=k == 3)
                    last.then_inc(unit_used, 1)
            rows_out(U_WOUT2, 4, HT, merged)

            transposes(4)
            ht_ready(4)
            wr = s_("router").rearrange("p (k n) -> p k n", k=KD)
            for tt in range(TT):
                for k in range(KD):
                    last = mm(psum[:, 4, tt * NR:(tt + 1) * NR], HT[:, k, tt * P:(tt + 1) * P], wr[:, k, :],
                              start=k == 0, stop=k == KD - 1)
            last.then_inc(lg_done, 1)
            pe.wait_ge(m_ready, 1)
            mm(psum[:, 5, 0:EXPERTS], stri, M[:, 0, :], start=True, stop=True)
            mm(psum[:, 5, EXPERTS:2 * EXPERTS], ones, M[:, 0, :], start=True, stop=False)
            mm(psum[:, 5, EXPERTS:2 * EXPERTS], stri, M[:, 1, :], start=False, stop=True)
            mm(psum[:, 5, 2 * EXPERTS:3 * EXPERTS], ones, M[:, 0, :], start=True, stop=False)
            mm(psum[:, 5, 2 * EXPERTS:3 * EXPERTS], ones, M[:, 1, :], start=False, stop=True).then_inc(rank_done, 1)
            pe.wait_ge(pg_ready, 1)
            for m in range(KD):
                if m >= 4:
                    pe.wait_ge(xs_dve, (m - 4) // 2 + 1)
                    pe.wait_ge(xs_act, (m - 4 + 1) // 2)
                for tt in range(TT):
                    last = mm(psum[:, m % 4, :], HN[:, tt, m * P:(m + 1) * P], PG[:, tt, :],
                              start=tt == 0, stop=tt == TT - 1)
                last.then_inc(xs_done, 1)
            pe.wait_ge(wp_ready, 1)
            for s in range(SB):
                for tt in range(TT):
                    last = nc.tensor.transpose(psum[:, 6 + s // 2, (s % 2) * S + tt * P:(s % 2) * S + (tt + 1) * P],
                                               WP[:, tt, s * P:(s + 1) * P], ident)
            last.then_inc(ct_done, 1)
            pe.wait_ge(ct_sb, 1)

            def expert_up(par, g, x, w, ks=range(KD)):
                for k in ks:
                    last = by_parts(psum[0:CH, par, g * D_EXP:(g + 1) * D_EXP], [v[:, k, :] for v in x],
                                    [v[:, k * D_EXP:(k + 1) * D_EXP] for v in w], k == 0, k == KD - 1)
                return last

            def expert_turn(par):
                for f in range(2):
                    last = nc.tensor.transpose(psum[:, 4 + par, f * CH:(f + 1) * CH], AT[0:CH, par, f * P:(f + 1) * P],
                                               ident[0:CH, 0:CH])
                return last

            def expert_down(par, x, w):
                for n in range(2):
                    for f in range(2):
                        a = f * D + n * 512
                        last = by_parts(psum[0:CH, (2, 6)[par] + n, :], [v[:, f, :] for v in x],
                                        [v[:, a:a + 512] for v in w], f == 0, f == 1)
                return last

            def experts(e, i=0):
                if e < EXPERTS - 1:
                    par = (e + 1) % 2
                    x = XWH[:, par], XWL[:, par]
                    pe.wait_ge(xw_lo, i * 2 + (e + 2))
                    expert_up(par, 0, x, parts(U_EXP + 2 + 3 * e, i)).then_inc(unit_used, 1)
                    w = parts(U_EXP + 3 + 3 * e, i)
                pe.wait_ge(at_ready, i * 2 + (e + 1))
                if e < EXPERTS - 1:
                    expert_up(par, 1, x, w, range(1))
                expert_turn(e % 2).then_inc(at_tr, 1)
                if e < EXPERTS - 1:
                    expert_up(par, 1, x, w, range(1, KD)).then_inc(unit_used, 1)
                pe.wait_ge(ae_lo, i * 2 + (e + 1))
                if e >= 2:
                    pe.wait_ge(y_copied, i * 2 + (e - 1))
                expert_down(e % 2, (AEH[:, e % 2], AEL[:, e % 2]),
                            parts(U_EXP + 4 + 3 * e if e < EXPERTS - 1 else UNITS - 1, i)).then_inc(unit_used, 1)

            pe.wait_ge(xw_lo, 1)
            for g in range(2):
                expert_up(0, g, (XWH[:, 0], XWL[:, 0]), parts(U_EXP + g)).then_inc(unit_used, 1)
            for e in range(4):
                experts(e)
            with pe.Fori(0, (EXPERTS - 6) // 2) as i:
                experts(4, i)
                experts(5, i)
            experts(EXPERTS - 2)
            experts(EXPERTS - 1)

            pe.wait_ge(tasks_ready, 1)
            total = pe.value_load(taski[0:1, 4 * TASKS:4 * TASKS + 1], min_val=0, max_val=TASKS)
            with pe.If(total > 0):
                pe.wait_ge(y_copied, EXPERTS)
                with pe.Fori(0, total) as t:
                    pe.wait_ge(more_loaded, t * 48 + 48)
                    pe.wait_ge(more_xw, t + 1)
                    expert_up(0, 0, (XW,), (ring[:, 0, :],))
                    expert_up(0, 1, (XW,), (ring[:, 1, :],)).then_inc(more_up, 1)
                    pe.wait_ge(tasks_ready, 1)
                    pe.wait_ge(more_at, t + 1)
                    expert_turn(0).then_inc(more_tr, 1)
                    pe.wait_ge(more_ae, t + 1)
                    expert_down(0, (AE,), (ring[:, 2, :],)).then_inc(unit_used, 1)
                    pe.wait_ge(more_copied, t + 1)
                pe.nop()
            pe.nop()

            pe.wait_ge(y_copied, EXPERTS - 1)
            for tt in range(TT):
                for s in range(SB):
                    pe.wait_ge(ys_loaded[s], 16)
                    for n in range(2):
                        last = mm(psum[:, 2 * tt + n, :], CT[:, s, tt * P:(tt + 1) * P],
                                  YS[:, s, n * 512:(n + 1) * 512], start=s == 0, stop=s == SB - 1)
                last.then_inc(y_done, 1)

        @block.scalar
        def _(act):
            step = Chain(act, act_steps)

            def sum_squares(event, parts, ready=None):
                act.wait_ge(squares_summed, event)
                at = 0
                for n, part in enumerate(parts):
                    if ready is not None:
                        act.wait_ge(x_ready, ready + n)
                    size = part.free_size()
                    if at + size > D:
                        step.sync()
                        at = 0
                    last = nc.scalar.activation(junk[:, at:at + size], part, ACT.Square,
                                                accum_out=ss[:, event, n:n + 1])
                    at += size
                    if n < len(parts) - 1:
                        step.mark(last)
                last.then_inc(squares_summed, 1)

            def norm(event, stage, ready=None):
                sum_squares(event, [X[:, tt, :] for tt in range(TT)], ready)
                act.wait_ge(rstd_ready, event + 1)
                nc.scalar.activation(HN[:, 1, :], X[:, 1, :], ACT.Copy, scale=rstd[:, event, 1:2]).then_inc(hn_act, 1)

            def take_transposes(stage, gain):
                for b in (1, 3):
                    act.wait_ge(tr_done, 4 * stage + b + 1)
                    for k in range(2):
                        last = nc.scalar.activation(HT[:, 2 * b + k, :], psum[:, b, k * S:(k + 1) * S], ACT.Copy,
                                                    scale=v_(gain, 2 * b + k))
                last.then_inc(ht_act, 1)

            def copy(out_, in_):
                return nc.scalar.activation(out_, in_, ACT.Copy)

            act.wait_ge(x_loaded, 16)
            norm(0, 0)
            act.wait_ge(vec_loaded, 16)
            take_transposes(0, "attn_pre")

            act.wait_ge(unit_used, U_PROJ + 3)
            copy(VF, proj_bank(2)).then_inc(evac_act, 1)
            act.wait_ge(evac_dve, 2)
            sum_squares(1, [CQ[:, 0, :], CQ[:, 1, :], CK[:, 0, 0:P], CK[:, 1, 0:P]])
            act.wait_ge(unit_used, U_PROJ + 4)
            copy(KA, psum[:, 3, 0:S])
            copy(VA, psum[:, 3, S:2 * S].rearrange("p (a b) -> p a b", a=TT)).then_inc(evac_act, 1)
            act.wait_ge(unit_used, U_PROJ + 6)
            copy(QA[:, 2:4, :], proj_bank(5)).then_inc(evac_act, 1)
            act.wait_ge(fz_ready, 1)
            step(nc.scalar.activation(fexp, fabs, ACT.Exp, scale=-1.0))
            nc.scalar.activation(flog, fexp, ACT.Ln, bias=1.0).then_inc(flog_ready, 1)
            act.wait_ge(unit_used, U_PROJ + 8)
            copy(KF, proj_bank(7)).then_inc(evac_act, 1)
            act.wait_ge(lat_up, 1)
            for tt in range(TT):
                q = psum[:, 2 + tt, 0:MLA_HEADS * MLA_QK].rearrange("p (h n) -> p h n", h=MLA_HEADS)
                copy(QM[:, tt, :, 0:NOPE], q[:, :, 0:NOPE])
                last = copy(QR[:, tt, 0:MLA_HEADS, :], q[:, :, NOPE:MLA_QK])
            last.then_inc(q_split, 1)
            act.wait_ge(qk_tr, 1)
            for tt in range(TT):
                last = copy(KMT[0:MLA_QK, :, tt * P:(tt + 1) * P],
                            psum[0:MLA_QK, 2 + tt, :].rearrange("p (h n) -> p h n", h=MLA_HEADS))
            last.then_inc(kmt_sb, 1)

            for h in range(HEADS):
                act.wait_ge(mx_ready, h + 1)
                nc.scalar.activation(SM[:, h % NS, 0:P + 1], SM[:, h % NS, 0:P + 1], ACT.Exp,
                                     bias=nmax[:, h, 0:1], accum_out=psums[:, h, 0:1])
                nc.scalar.activation(SM[:, h % NS, P + 1:P + S + 2], SM[:, h % NS, P + 1:P + S + 2], ACT.Exp,
                                     bias=nmax[:, h, 1:2], accum_out=psums[:, h, 1:2]).then_inc(exp_done, 1)

            act.wait_ge(o_sb, HEADS // 4)
            spans = (slice(0, 512), slice(512, 768), slice(768, 1024))
            sum_squares(2, [O[:, tt, sp_] for sp_ in spans for tt in range(TT)])
            act.wait_ge(rstd_ready, 3)
            for g, sp_ in enumerate(spans):
                last = nc.scalar.activation(HN[:, 1, sp_], O[:, 1, sp_], ACT.Copy, scale=rstd[:, 2, 2 * g + 1:2 * g + 2])
            last.then_inc(hn_act, 1)
            take_transposes(1, "group")
            for n in range(2):
                split_hi(act, U_FFN + n)
            act.wait_ge(unit_used, U_FFN)
            sum_squares(3, [psum[:, 4 + 2 * tt:6 + 2 * tt, :].rearrange("p a b -> p (a b)") for tt in range(TT)])

            norm(4, 2, 1)
            for b in range(KD // 2):
                act.wait_ge(tr_done, 4 * 2 + b + 1)
                for k in range(2):
                    last = nc.scalar.activation(HTH[:, 2 * b + k, :], psum[:, b, k * S:(k + 1) * S], ACT.Copy,
                                                scale=v_("ffn_pre", 2 * b + k))
                last.then_inc(ht_hi, 1)
            c0, cb = VC["conv"].start, VC["conv_b"].start

            def ffn(c, i=0):
                if c < FF_CHUNKS - 1:
                    split_hi(act, U_FFN + 2 + 3 * c, i)
                act.wait_ge(unit_used, i * 6 + (U_FFN + 1 + 3 * c if c else U_FFN + 2))
                for g in range(2):
                    for f in range(2):
                        at = i * 4 + (2 * c + g * FF_TILES + f)
                        last = nc.scalar.activation(
                            U[:, c % 2, 2 * g + f, :], psum[:, 2 * (c % 2) + g, f * S:(f + 1) * S], ACT.Identity,
                            bias=vec[:, ds(at + cb, 1)], scale=vec[:, ds(at + (c0 + 2 * 2 * FF_TILES), 1)])
                    last.then_inc(tap_last, 1)
                if c < FF_CHUNKS - 1:
                    split_hi(act, U_FFN + 3 + 3 * c, i)
                act.wait_ge(gate_conv, i * 2 + (c + 1))
                nc.scalar.activation(G[:, c % 2], U[:, c % 2, 0:2, :], ACT.Gelu_apprx_tanh).then_inc(gelu_done, 1)
                split_hi(act, U_FFN + 4 + 3 * c if c < FF_CHUNKS - 1 else U_GLA - 1, i)

            ffn(0)
            ffn(1)
            with act.Fori(0, (FF_CHUNKS - 3) // 2) as i:
                ffn(2, i)
                ffn(3, i)
            ffn(FF_CHUNKS - 1)
            act.wait_ge(unit_used, U_GLA)
            sum_squares(5, [psum[:, 4 + 2 * tt:6 + 2 * tt, :].rearrange("p a b -> p (a b)") for tt in range(TT)])

            norm(6, 3, 3)
            take_transposes(3, "norm1")
            act.wait_ge(al_done, 1)
            copy(AL[0:GLA_RANK, :], psum[0:GLA_RANK, 4, 0:S]).then_inc(al_sb, 1)
            act.wait_ge(z_abs, 1)
            step(nc.scalar.activation(zexp, zabs, ACT.Exp, scale=-1.0))
            nc.scalar.activation(zabs, zexp, ACT.Ln, bias=1.0).then_inc(z_log, 1)
            for j in range(2):
                act.wait_ge(unit_used, U_GLA + 3 + j)
                copy(V[:, :, j * S:(j + 1) * S], proj_bank(2 + j)).then_inc(v_sb, 1)
            act.wait_ge(bc_done, 1)
            step.mark(copy(BC, psum[:, 4, :].rearrange("p (a b) -> p a b", a=2)))
            nc.scalar.activation(EB, psum[:, 4, :].rearrange("p (a b) -> p a b", a=2), ACT.Exp)
            nc.scalar.activation(ENB, psum[:, 4, :].rearrange("p (a b) -> p a b", a=2), ACT.Exp, scale=-1.0)
            step.sync()
            for f in range(2):
                for n in range(S // GLA_CHUNK):
                    a, b = n * GLA_CHUNK, (n + 1) * GLA_CHUNK
                    nc.scalar.activation(KE[:, f, a:b], BC[:, f, a:b], ACT.Exp, bias=BC[:, f, b - 1:b], scale=-1.0)
                last = nc.scalar.activation(DEC[:, f, :], BC[:, f, GLA_CHUNK - 1:S:GLA_CHUNK], ACT.Exp)
            last.then_inc(exps_done, 1)
            for j in range(2):
                act.wait_ge(unit_used, U_GLA + 5 + j)
                copy(UP[:, 2 * j:2 * j + 2, PAD:PAD + S], proj_bank(6 + j)).then_inc(pool_in, 1)
            act.wait_ge(kend_tr, 1)
            copy(KET, proj_bank(0)).then_inc(kend_sb, 1)
            act.wait_ge(o_done, 2)
            sum_squares(7, [psum[:, b, n * P:(n + 1) * P] for b in (1, 4) for n in range(4)])
            for j in range(2):
                act.wait_ge(unit_used, U_GLA + 7 + j)
                nc.scalar.activation(RS[:, 2 * j:2 * j + 2, :], proj_bank(6 + j), ACT.Silu).then_inc(g_act, 1)
            for dst, first in ((SG, 8), (SP, 12)):
                for j in range(4):
                    act.wait_ge(unit_used, U_GLA + first + j + 1)
                    nc.scalar.activation(dst[:, 2 * j:2 * j + 2, :], proj_bank((2, 3, 0, 5)[j]),
                                         ACT.Sigmoid).then_inc(g_act, 1)

            act.wait_ge(merged, 4)
            for n in range(2):
                split_hi(act, U_EXP + n)
            norm(8, 4, 5)
            take_transposes(4, "norm2")
            act.wait_ge(top_in, 1)
            nc.scalar.activation(g4b, g4a, ACT.Exp).then_inc(top_exp, 1)
            act.wait_ge(top_e, 1)
            nc.scalar.activation(col[:, 4, :], col[:, 3, :], ACT.Exp).then_inc(top_eexp, 1)
            for m in (1, 3, 5, 7):
                act.wait_ge(xs_done, m + 1)
                nc.scalar.activation(XS[:, m, 0:SLOTS], psum[:, m % 4, :], ACT.Copy,
                                     scale=v_("norm2", m)).then_inc(xs_act, 1)

            def window(dst, at):
                return copy(dst, XS[:, :, ds(at, CH)])

            def window_hi(e, i=0):
                at = act.value_load(starti[0:1, ds(i * 2 + e, 1)], min_val=0, max_val=SLOTS)
                window(XWH[:, e % 2], at).then_inc(xw_hi, 1)

            def silu(par):
                return nc.scalar.activation(SL[0:CH, par], psum[0:CH, par, 0:D_EXP], ACT.Silu)

            def results(e, i=0):
                act.wait_ge(unit_used, i * 6 + (U_EXP + 5 + 3 * e if e < EXPERTS - 1 else UNITS))
                if e >= 2:
                    act.wait_ge(y_stored, i * 32 + 16 * (e - 1))
                b = (2, 6)[e % 2]
                copy(YO[0:CH, e % 2, :], psum[0:CH, b:b + 2, :].rearrange("p a b -> p (a b)")).then_inc(y_copied, 1)

            def experts(e, i=0):
                if e < EXPERTS - 1:
                    split_hi(act, U_EXP + 2 + 3 * e, i)
                act.wait_ge(unit_used, i * 6 + (U_EXP + 2 if e == 0 else U_EXP + 1 + 3 * e))
                silu(e % 2).then_inc(silu_done, 1)
                if e < EXPERTS - 1:
                    split_hi(act, U_EXP + 3 + 3 * e, i)
                if e >= 1:
                    results(e - 1, i)
                if e < EXPERTS - 2:
                    window_hi(e + 2, i)
                split_hi(act, U_EXP + 4 + 3 * e if e < EXPERTS - 1 else UNITS - 1, i)
                act.wait_ge(at_tr, i * 2 + (e + 1))
                copy(AEH[:, e % 2], psum[:, 4 + e % 2, 0:2 * CH].rearrange("p (f n) -> p f n", f=2)).then_inc(ae_hi, 1)

            act.wait_ge(pad_zero, 1)
            act.wait_ge(xs_dve, 4)
            act.wait_ge(xs_act, 4)
            act.wait_ge(starts_ready, 1)
            for e in range(2):
                window_hi(e)
            for e in range(4):
                experts(e)
            with act.Fori(0, (EXPERTS - 6) // 2) as i:
                experts(4, i)
                experts(5, i)
            experts(EXPERTS - 2)
            experts(EXPERTS - 1)
            results(EXPERTS - 1)

            act.wait_ge(tasks_ready, 1)
            total = act.value_load(taski[0:1, 4 * TASKS:4 * TASKS + 1], min_val=0, max_val=TASKS)
            with act.If(total > 0):
                with act.Fori(0, total) as t:
                    at = act.value_load(taski[0:1, ds(t + 3 * TASKS, 1)], min_val=0, max_val=SLOTS)
                    window(XW, at).then_inc(more_xw, 1)
                    act.wait_ge(more_up, t + 1)
                    silu(0).then_inc(more_silu, 1)
                act.nop()
            act.nop()
            for tt in range(TT):
                act.wait_ge(final_x, tt + 1)
                sum_squares(9 + tt, [X[:, tt, :]])

        @block.gpsimd
        def _(pool):
            nc.gpsimd.memset(neghalf[:, :], -0.5).then_inc(pool_steps, 1)
            pool.wait_ge(pool_steps, 1)
            steps = 1

            def inverse_roots(event, n):
                pool.wait_ge(ms_ready, event + 1)
                nc.gpsimd.tensor_tensor(rstd[:, event, 0:n], ms[:, event, 0:n], neghalf[:, 0:n],
                                        ALU.pow).then_inc(rstd_ready, 1)

            inverse_roots(0, 2)
            pool.wait_ge(line_sb, 1)
            pool.dma_start(line_dram, line[0:SWA_HEADS, :].unsqueeze(1).to_broadcast([SWA_HEADS, P, P + S])
                           ).then_inc(line_stored, 16)
            pool.wait_ge(line_stored, 16)
            for a, n, first in ((0, P, P + P - 1), (P, S, P - 1)):
                src = bass.AP(line_dram.tensor, first, [[P + S - 1, P], [P * (P + S), SWA_HEADS], [1, n]])
                pool.dma_start(bias[:, :, a:a + n], src).then_inc(bias_loaded, 16)
            for event, n in ((1, 4), (2, 6), (3, 2), (4, 2)):
                inverse_roots(event, n)

            def activations(c, i=0):
                pool.wait_ge(gelu_done, i * 2 + (c + 1))
                pool.wait_ge(up_conv, i * 2 + (c + 1))
                up = U[:, c % 2, 2:4, :]
                nc.gpsimd.tensor_tensor(AF[:, c % 2], G[:, c % 2], up, MUL).then_inc(af_parts, 1)
                nc.gpsimd.tensor_tensor(AFH[:, c % 2], G[:, c % 2], up, MUL).then_inc(af_parts, 1)
                pool.wait_ge(af_parts, i * 4 + 2 * (c + 1))
                nc.gpsimd.tensor_tensor(AFL[:, c % 2], AF[:, c % 2], AFH[:, c % 2].bitcast(fp32), SUB
                                        ).then_inc(act_ready, 1)

            with pool.Fori(0, FF_CHUNKS // 2) as i:
                activations(0, i)
                activations(1, i)
            activations(FF_CHUNKS - 1)
            for event, n in ((5, 2), (6, 2)):
                inverse_roots(event, n)
            pool.wait_ge(pool_zero, 1)
            pool.wait_ge(pool_in, 2)
            t0 = PAD
            for n, (dst, src, g) in enumerate(((PA, UP, 0), (PB, PA, 1), (PA, PB, 2), (PB, PA, 3))):
                shift = 1 << n
                last = nc.gpsimd.tensor_tensor(dst[:, g:, t0:], src[:, g:, t0:], src[:, g:, t0 - shift:PAD + S - shift],
                                               ADD)
                if n < 3:
                    last.then_inc(pool_steps, 1)
                    steps += 1
                    pool.wait_ge(pool_steps, steps)
            last.then_inc(pool_sums, 1)
            for event, n in ((7, 8), (8, 2)):
                inverse_roots(event, n)

            def window_lo(e, i=0):
                at = pool.value_load(starti[0:1, ds(i * 2 + e, 1)], min_val=0, max_val=SLOTS)
                pool.wait_ge(xw_hi, i * 2 + (e + 1))
                nc.gpsimd.tensor_tensor(XWL[:, e % 2], XS[:, :, ds(at, CH)], XWH[:, e % 2].bitcast(fp32), SUB
                                        ).then_inc(xw_lo, 1)

            def experts(e, i=0):
                if e < EXPERTS - 2:
                    window_lo(e + 2, i)
                at = pool.value_load(starti[0:1, ds(i * 2 + e, 1)], min_val=0, max_val=SLOTS)
                pool.wait_ge(y_copied, i * 2 + (e + 1))
                if e >= 1:
                    pool.wait_ge(y_stored, i * 32 + 16 * e)
                pool.dma_start(results_dram[ds(at, CH)], YO[0:CH, e % 2, :]).then_inc(y_stored, 16)

            pool.wait_ge(starts_ready, 1)
            for e in range(2):
                window_lo(e)
            experts(0)
            experts(1)
            with pool.Fori(0, (EXPERTS - 4) // 2) as i:
                experts(2, i)
                experts(3, i)
            experts(EXPERTS - 2)
            experts(EXPERTS - 1)
            pool.wait_ge(y_stored, 16 * EXPERTS)

            pool.wait_ge(tasks_ready, 1)
            total = pool.value_load(taski[0:1, 4 * TASKS:4 * TASKS + 1], min_val=0, max_val=TASKS)
            with pool.If(total > 0):
                with pool.Fori(0, total) as t:
                    at = pool.value_load(taski[0:1, ds(t + 3 * TASKS, 1)], min_val=0, max_val=SLOTS)
                    pool.wait_ge(more_copied, t + 1)
                    pool.dma_start(results_dram[ds(at, CH)], YO[0:CH, 0, :]).then_inc(more_stored, 16)
                    pool.wait_ge(more_stored, t * 16 + 16)
                pool.nop()
            pool.nop()
            nc.gpsimd.memset(neghalf[:, :], -0.5).then_inc(results_in_dram, 1)
            pool.wait_ge(results_in_dram, 1)
            for tt in range(TT):
                inverse_roots(9 + tt, 1)

        @block.vector
        def _(dve):
            step = Chain(dve, dve_steps)
            V_ = nc.vector
            tt_op, ts_op, stt = V_.tensor_tensor, V_.tensor_scalar, V_.scalar_tensor_tensor

            def mean_squares(event, parts):
                dve.wait_ge(squares_summed, event + 1)
                for a, b, n in parts:
                    last = ts_op(ms[:, event, a:b], ss[:, event, a:b], 1.0 / n, EPS, MUL, ADD)
                last.then_inc(ms_ready, 1)
                dve.wait_ge(rstd_ready, event + 1)

            def norm(event):
                mean_squares(event, [(0, 2, D)])
                ts_op(HN[:, 0, :], X[:, 0, :], rstd[:, event, 0:1], None, MUL).then_inc(hn_dve, 1)

            def take_transposes(stage, gain):
                for b in (0, 2):
                    dve.wait_ge(tr_done, 4 * stage + b + 1)
                    for k in range(2):
                        last = ts_op(HT[:, 2 * b + k, :], psum[:, b, k * S:(k + 1) * S], v_(gain, 2 * b + k), None, MUL)
                last.then_inc(ht_dve, 1)

            def add_branch(event, row):
                mean_squares(event, [(0, 2, D)])
                for tt in range(TT):
                    stt(T2[:, tt, :], psum[:, 4 + 2 * tt:6 + 2 * tt, :].rearrange("p a b -> p (a b)"),
                        rstd[:, event, tt:tt + 1], r_(row), MUL, MUL).then_inc(t2_ready, 1)
                for tt in range(TT):
                    dve.wait_ge(t2_ready, 2 * (event == 5) + tt + 1)
                    tt_op(X[:, tt, :], X[:, tt, :], T2[:, tt, :], ADD).then_inc(x_ready, 1)

            dve.wait_ge(x_loaded, 16)
            norm(0)
            dve.wait_ge(vec_loaded, 16)
            take_transposes(0, "attn_pre")
            dve.wait_ge(const_loaded, 16)
            dve.wait_ge(line_done, 1)
            tt_op(line[0:SWA_HEADS, :], psum[0:SWA_HEADS, 4, 0:P + S], c_("line")[0:SWA_HEADS, :], ADD).then_inc(line_sb, 1)

            dve.wait_ge(unit_used, U_PROJ + 1)
            V_.tensor_copy(CQ, proj_bank(0)).then_inc(evac_dve, 1)
            dve.wait_ge(unit_used, U_PROJ + 2)
            V_.tensor_copy(CK, proj_bank(1)[:, :, 0:164]).then_inc(evac_dve, 1)
            dve.wait_ge(evac_dve, 2)
            dve.wait_ge(rows_loaded, 16)
            step(tt_op(fz, CK[:, :, 160:164], r_("forget").unsqueeze(1).to_broadcast([P, TT, FOX_HEADS]), ADD))
            stt(fabs, fz, -1.0, fz, MUL, MAX).then_inc(fz_ready, 1)
            mean_squares(1, [(0, 2, Q_RANK), (2, 4, KV_RANK)])
            for tt in range(TT):
                ts_op(CQ[:, tt, :], CQ[:, tt, :], rstd[:, 1, tt:tt + 1], None, MUL)
                last = ts_op(CK[:, tt, 0:P], CK[:, tt, 0:P], rstd[:, 1, 2 + tt:3 + tt], None, MUL)
            last.then_inc(lat_hn, 1)
            dve.wait_ge(unit_used, U_PROJ + 5)
            V_.tensor_copy(QA[:, 0:2, :], proj_bank(4)).then_inc(evac_dve, 1)
            dve.wait_ge(flog_ready, 1)
            stt(flf, fz, 0.0, flog, MIN, SUB).then_inc(flf_ready, 1)
            dve.wait_ge(unit_used, U_PROJ + 7)
            V_.tensor_copy(QF, proj_bank(6)).then_inc(evac_dve, 1)
            dve.wait_ge(lat_tr, 1)
            for k in range(2):
                ts_op(CQT[:, k, :], psum[:, 0, k * S:(k + 1) * S], v_("q_lat", k), None, MUL)
            ts_op(CKT, psum[:, 1, 0:S], v_("kv_lat", 0), None, MUL).then_inc(lat_ct, 1)
            dve.wait_ge(ft_done, 1)
            V_.tensor_copy(FT[0:FOX_HEADS, :], psum[0:FOX_HEADS, 6, 0:S]).then_inc(ft_sb, 1)
            V_.tensor_copy(QR[:, :, MLA_HEADS, :], CK[:, :, P:P + ROPE])
            dve.wait_ge(lat_up, 1)
            for tt in range(TT):
                kv = psum[:, 4 + tt, :].rearrange("p (h n) -> p h n", h=MLA_HEADS)
                V_.tensor_copy(KM[:, tt, :, 0:NOPE], kv[:, :, 0:NOPE])
                last = V_.tensor_copy(VM[:, tt], kv[:, :, NOPE:])
            step(last)
            dve.wait_ge(q_split, 1)
            nh = MLA_HEADS + 1
            lo, hi = QR[:, :, :, 0:HALF], QR[:, :, :, HALF:ROPE]
            r4 = [rot[:, q].rearrange("p t (h n) -> p t h n", h=nh) for q in range(4)]
            cs, sn = (c_(k).rearrange("p (t n) -> p t n", t=TT).unsqueeze(2).to_broadcast([P, TT, nh, HALF])
                      for k in ("cos", "sin"))
            for q, (part, trig) in enumerate(((lo, cs), (hi, sn), (lo, sn), (hi, cs))):
                step.mark(tt_op(r4[q], part, trig, MUL))
            step.sync()
            for n, (x1, x2, op) in enumerate(((r4[0], r4[1], SUB), (r4[2], r4[3], ADD))):
                at = NOPE + n * HALF
                tt_op(QM[:, :, :, at:at + HALF], x1[:, :, 0:MLA_HEADS], x2[:, :, 0:MLA_HEADS], op)
                for tt in range(TT):
                    last = tt_op(KM[:, tt, :, at:at + HALF],
                                 x1[:, tt, MLA_HEADS:nh].to_broadcast([P, MLA_HEADS, HALF]),
                                 x2[:, tt, MLA_HEADS:nh].to_broadcast([P, MLA_HEADS, HALF]), op)
            last.then_inc(qk_rot, 1)
            dve.wait_ge(qk_tr, 1)
            for tt in range(TT):
                last = V_.tensor_copy(QMT[0:MLA_QK, :, tt * P:(tt + 1) * P],
                                      psum[0:MLA_QK, tt, :].rearrange("p (h n) -> p h n", h=MLA_HEADS))
            last.then_inc(qmt_sb, 1)

            def take_probs(h):
                dve.wait_ge(pt_done, h + 1)
                if h >= 2:
                    dve.wait_ge(pv_done, h - 1)
                V_.tensor_copy(PT[:, h % 2], psum[:, 6 + h % 2, 0:3 * P].rearrange("p (a b) -> p a b", a=3)).then_inc(pt_sb, 1)

            def take_outputs(g):
                dve.wait_ge(pv_done, 4 * g + 4)
                step(V_.reciprocal(rsum[:, 4 * g:4 * g + 4, :], psums[:, 4 * g:4 * g + 4, :]))
                src = psum[:, 2 + g % 2, :].rearrange("p (h t n) -> p h t n", h=4, t=TT)
                for tt in range(TT):
                    last = tt_op(O[:, tt, 4 * g * HD:(4 * g + 4) * HD].rearrange("p (h n) -> p h n", h=4), src[:, :, tt, :],
                                 rsum[:, 4 * g:4 * g + 4, tt:tt + 1].to_broadcast([P, 4, HD]), MUL)
                last.then_inc(o_sb, 1)

            dve.wait_ge(bias_loaded, 32)
            for h in range(HEADS):
                b = SM[:, h % NS, :]
                if h >= NS:
                    dve.wait_ge(pt_done, h - NS + 1)
                ends = b[:, 0:P + S + 2:P + S + 1]
                if h < SWA_HEADS:
                    V_.tensor_copy(ends, r_("sinks")[:, h:h + 1].to_broadcast([P, 2]))
                else:
                    V_.memset(ends, NEG)
                dve.wait_ge(s_done, h + 1)
                scale = HD ** -0.5 if h < SWA_HEADS + FOX_HEADS else MLA_QK ** -0.5
                stt(b[:, 1:P + S + 1], psum[:, 4 + h % 2, 0:P + S], scale, bias[:, h, :] if h < SWA_HEADS else causal,
                    MUL, ADD).then_inc(s_read, 1)
                dve.wait_ge(s_read, h + 1)
                V_.tensor_reduce(nmax[:, h, 0:1], b[:, 0:P + 1], AX.X, MAX, negate=True)
                V_.tensor_reduce(nmax[:, h, 1:2], b[:, P + 1:P + S + 2], AX.X, MAX, negate=True).then_inc(mx_ready, 1)
                if h >= 1:
                    take_probs(h - 1)
                if h % 4 == 1 and h >= 5:
                    take_outputs(h // 4 - 1)
            take_probs(HEADS - 1)
            take_outputs(HEADS // 4 - 1)

            mean_squares(2, [(0, 2, 512), (2, 6, 256)])
            dve.wait_ge(o_sb, HEADS // 4)
            for g, (a, b) in enumerate(((0, 512), (512, 768), (768, 1024))):
                last = ts_op(HN[:, 0, a:b], O[:, 0, a:b], rstd[:, 2, 2 * g:2 * g + 1], None, MUL)
            last.then_inc(hn_dve, 1)
            take_transposes(1, "group")
            for n in range(2):
                split_lo(dve, U_FFN + n)
            add_branch(3, "attn_post")

            dve.wait_ge(x_ready, 2)
            norm(4)
            for b in range(KD // 2):
                dve.wait_ge(ht_hi, b + 1)
                for k in (2 * b, 2 * b + 1):
                    last = stt(HTL[:, k, :], psum[:, b, (k % 2) * S:(k % 2 + 1) * S], v_("ffn_pre", k),
                               HTH[:, k, :].bitcast(fp32), MUL, SUB)
                last.then_inc(ht_lo, 1)
            c0 = VC["conv"].start

            def ffn(c, i=0):
                if c < FF_CHUNKS - 1:
                    split_lo(dve, U_FFN + 2 + 3 * c, i)
                for g in range(2):
                    dve.wait_ge(tap_last, i * 4 + (2 * c + 1 + g))
                    for back in (1, 2):
                        for f in range(2):
                            at = i * 4 + (2 * c + g * FF_TILES + f)
                            u = U[:, c % 2, 2 * g + f, back:S]
                            ins = stt(u, psum[:, 2 * (c % 2) + g, f * S:(f + 1) * S - back],
                                      vec[:, ds(at + (c0 + (2 - back) * 2 * FF_TILES), 1)], u, MUL, ADD)
                            if back == 2 and f == 1:
                                ins.then_inc(gate_conv if g == 0 else up_conv, 1)
                            else:
                                step.mark(ins)
                        if back == 1:
                            step.sync()
                if c < FF_CHUNKS - 1:
                    split_lo(dve, U_FFN + 3 + 3 * c, i)
                split_lo(dve, U_FFN + 4 + 3 * c if c < FF_CHUNKS - 1 else U_GLA - 1, i)

            ffn(0)
            ffn(1)
            at0 = step.n
            with dve.Fori(0, (FF_CHUNKS - 3) // 2) as i:
                step.extra = i * 12
                ffn(2, i)
                ffn(3, i)
                assert step.n - at0 == 12
            step.n, step.extra = at0 + 12 * ((FF_CHUNKS - 3) // 2), 0
            ffn(FF_CHUNKS - 1)
            add_branch(5, "ffn_post")

            dve.wait_ge(x_ready, 4)
            norm(6)
            take_transposes(3, "norm1")
            V_.memset(QZ, 0.0)
            V_.memset(ST, 0.0)
            for t_ in (UP, PA, PB):
                last = V_.memset(t_[:, :, 0:PAD], 0.0)
            last.then_inc(pool_zero, 1)
            dve.wait_ge(pool_zero, 1)
            dve.wait_ge(z_done, 1)
            step(tt_op(z2, psum[:, 5, :].rearrange("p (a b) -> p a b", a=TT),
                       r_("b_alpha").unsqueeze(1).to_broadcast([P, TT, GLA_KEY]), ADD))
            stt(zabs, z2, -1.0, z2, MUL, MAX).then_inc(z_abs, 1)
            dve.wait_ge(z_log, 1)
            step(stt(z2, z2, 0.0, zabs, MIN, SUB))
            ts_op(LA, z2, 1.0 / GATE_NORMALIZER, None, MUL).then_inc(la_ready, 1)
            dve.wait_ge(exps_done, 1)
            dve.wait_ge(unit_used, U_GLA + 2)
            step(stt(QD, proj_bank(0), GLA_DK ** -0.5, EB, MUL, MUL))
            for c in range(2):
                a = c * GLA_CHUNK
                last = V_.tensor_copy(QZ[:, :, :, c, a:a + GLA_CHUNK],
                                      QD.rearrange("p f (t n) -> p f t n", t=TT)[:, :, :, a:a + GLA_CHUNK])
            last.then_inc(g_dve, 1)
            tt_op(KDE, proj_bank(1), ENB, MUL)
            tt_op(KEND, proj_bank(1), KE, MUL).then_inc(g_dve, 1)
            mask = btri.bitcast(i32).unsqueeze(1).to_broadcast([P, 2, P])
            for odd in range(2):
                dve.wait_ge(st_done, odd + 1)
                for tt in range(TT):
                    last = V_.copy_predicated(ST[:, tt, odd::2, :], mask,
                                              psum[:, (1, 4)[odd], tt * S:(tt + 1) * S].rearrange("p (f n) -> p f n", f=2))
                last.then_inc(st_sb, 1)
            for n in range(3):
                dve.wait_ge(inc_done, n + 1)
                for f in range(2):
                    inc = psum[:, (2, 3, 5)[n], f * S:(f + 1) * S]
                    if n == 0:
                        last = V_.tensor_copy(SS[:, 0, f, :], inc)
                    else:
                        last = stt(SS[:, n, f, :], SS[:, n - 1, f, :], DEC[:, f, n:n + 1], inc, MUL, ADD)
                last.then_inc(states_ready, 1)
                dve.wait_ge(states_ready, n + 1)
            mean_squares(7, [(0, 8, GLA_DV)])
            for odd in range(2):
                for tt in range(TT):
                    at = 4 * odd + 2 * tt
                    last = tt_op(OHN[:, tt, :].rearrange("p (h n) -> p h n", h=GLA_HEADS)[:, odd::2, :],
                                 psum[:, (1, 4)[odd], tt * S:(tt + 1) * S].rearrange("p (f n) -> p f n", f=2),
                                 rstd[:, 7, at:at + 2].unsqueeze(2).to_broadcast([P, 2, P]), MUL)
                last.then_inc(ohn_ready, 1)
            dve.wait_ge(pool_sums, 1)
            for g, w in enumerate(POOL_WINDOWS):
                src = PA if g % 2 == 0 else PB
                stt(PM[:, g, PAD:], src[:, g, 2 * PAD:], 1.0 / w, UP[:, g, 2 * PAD:], MUL, SUB)
                step.mark(tt_op(PM[:, g, 0:PAD], src[:, g, PAD:2 * PAD],
                                c_("rcount").rearrange("p (g n) -> p g n", g=POOL_G)[:, g, :], MUL))
            step.sync()
            tt_op(PM[:, :, 0:PAD], PM[:, :, 0:PAD], UP[:, :, PAD:2 * PAD], SUB).then_inc(pm_ready, 1)
            dve.wait_ge(pool_done, 1)
            for g in range(POOL_G):
                last = ts_op(YP[:, g, :], psum[:, 6 + g // 2, (g % 2) * S:(g % 2 + 1) * S], v_("pool_scale", g), None, MUL)
            last.then_inc(yp_sb, 1)
            dve.wait_ge(ot_tr, 1)
            dve.wait_ge(g_act, 2)
            for k in range(4):
                last = stt(OT[:, k, :], psum[:, (1, 4)[k // 2], (k % 2) * S:(k % 2 + 1) * S], v_("gla", k),
                           RS[:, k, :], MUL, MUL)
            last.then_inc(ot_sb, 1)
            dve.wait_ge(g_act, 10)
            for j in range(2):
                dve.wait_ge(unit_used, U_BRANCH + 2 * j + 2)
                for hf in range(2):
                    m = 4 * j + 2 * hf
                    step.mark(tt_op(T1a, proj_bank((6, 2)[j] + hf), SG[:, m:m + 2, :], MUL))
                    step(tt_op(T1b, proj_bank((4, 0)[j] + hf), SP[:, m:m + 2, :], MUL))
                    tt_op(HT[:, m:m + 2, :], T1a, T1b, ADD).then_inc(merged, 1)
                    dve.wait_ge(merged, 2 * j + hf + 1)
            for n in range(2):
                split_lo(dve, U_EXP + n)
            dve.wait_ge(unit_used, U_EXP)
            for tt in range(TT):
                tt_op(X[:, tt, :], X[:, tt, :], psum[:, 4 + 2 * tt:6 + 2 * tt, :].rearrange("p a b -> p (a b)"), ADD
                      ).then_inc(x_ready, 1)

            dve.wait_ge(x_ready, 6)
            norm(8)
            take_transposes(4, "norm2")
            dve.wait_ge(lg_done, 1)
            step(tt_op(LG, psum[:, 4, 0:TT * NR].rearrange("p (a b) -> p a b", a=TT),
                       r_("router_b").unsqueeze(1).to_broadcast([P, TT, NR]), ADD))

            def by_group(v):
                return v.rearrange("p (g e) -> p g e", g=GROUPS)

            def spread(v, n):
                return v.unsqueeze(2).to_broadcast([P, TT, n])

            def first_max(onehot, eq, cand, values, maximum, index, n):
                step(V_.tensor_reduce(maximum, values, AX.X, MAX))
                step(tt_op(eq, values, spread(maximum, n), EQ))
                step(stt(cand, eq, -1000.0, iota[:, 0:n].unsqueeze(1).to_broadcast([P, TT, n]), MUL, ADD))
                step(V_.tensor_reduce(index, cand, AX.X, MIN))
                step(tt_op(onehot, cand, spread(index, n), EQ))

            gmax, gidx, e1, dlt, ex, gp, den, w1, w2, e2, idx, d1, d2 = (col[:, n, :] for n in
                                                                         (0, 1, 2, 3, 4, 5, 6, 7, 8, 9, 10, 11, 12))
            first_max(g4d, g4b, g4c, LG[:, :, 0:GROUPS], gmax, gidx, GROUPS)
            tt_op(g4a, LG[:, :, 0:GROUPS], spread(gmax, GROUPS), SUB).then_inc(top_in, 1)
            for tt in range(TT):
                step.mark(tt_op(by_group(EM[:, tt]), by_group(LG[:, tt, GROUPS:NR]),
                                g4d[:, tt, :].unsqueeze(2).to_broadcast([P, GROUPS, PER_GROUP]), MUL))
            step(ts_op(g4c, g4d, 1.0, -NEG, SUB, MUL))
            for tt in range(TT):
                step.mark(tt_op(by_group(EM[:, tt]), by_group(EM[:, tt]),
                                g4c[:, tt, :].unsqueeze(2).to_broadcast([P, GROUPS, PER_GROUP]), ADD))
            step.sync()
            first_max(OH1, EQX, CAND, EM, e1, idx, EXPERTS)
            step(stt(EM, OH1, 2 * NEG, EM, MUL, ADD))
            first_max(OH2, EQX, CAND, EM, e2, idx, EXPERTS)
            tt_op(M, OH1, OH2, ADD).then_inc(m_ready, 1)
            tt_op(dlt, e2, e1, SUB).then_inc(top_e, 1)
            dve.wait_ge(top_exp, 1)
            step(V_.tensor_reduce(gp, g4b, AX.X, ADD))
            dve.wait_ge(top_eexp, 1)
            step(ts_op(den, ex, 1.0, None, ADD))
            step(tt_op(den, den, gp, MUL))
            step(V_.reciprocal(w1, den))
            step(tt_op(w2, w1, ex, MUL))

            dve.wait_ge(rank_done, 1)
            step(V_.tensor_copy(CNT, psum[:, 5, 2 * EXPERTS:3 * EXPERTS]))
            step(V_.tensor_tensor_scan(CUM, ones[:, 0:EXPERTS], CNT, 0.0, MUL, ADD))
            step(tt_op(START, CUM, CNT, SUB))
            step(tt_op(RK, psum[:, 5, 0:2 * EXPERTS].rearrange("p (a b) -> p a b", a=TT),
                       START.unsqueeze(1).to_broadcast([P, TT, EXPERTS]), ADD))
            for oh, d in ((OH1, d1), (OH2, d2)):
                step(tt_op(PR, oh, RK, MUL))
                step(V_.tensor_reduce(d, PR, AX.X, ADD))
            for tt in range(TT):
                step.mark(ts_op(PG[:, tt, :], iota, d1[:, tt:tt + 1], None, EQ))
            step.sync()
            for tt in range(TT):
                last = stt(PG[:, tt, :], iota, d2[:, tt:tt + 1], PG[:, tt, :], EQ, ADD)
            last.then_inc(pg_ready, 1)
            for tt in range(TT):
                step.mark(ts_op(WP[:, tt, :], iota, d1[:, tt:tt + 1], w1[:, tt:tt + 1], EQ, MUL))
                step.mark(ts_op(WQ[:, tt, :], iota, d2[:, tt:tt + 1], w2[:, tt:tt + 1], EQ, MUL))
            step.sync()
            tt_op(WP, WP, WQ, ADD).then_inc(wp_ready, 1)
            V_.memset(XS[:, :, SLOTS:], 0.0).then_inc(pad_zero, 1)
            V_.tensor_copy(starti[:, :], START).then_inc(starts_ready, 1)
            for m in (0, 2, 4, 6):
                dve.wait_ge(xs_done, m + 1)
                ts_op(XS[:, m, 0:SLOTS], psum[:, m % 4, :], v_("norm2", m), None, MUL).then_inc(xs_dve, 1)

            dve.wait_ge(ct_done, 1)
            for s in range(0, SB, 2):
                last = V_.tensor_copy(CT[:, s:s + 2, :], proj_bank(6 + s // 2))
            last.then_inc(ct_sb, 1)

            cnt_j = CNT.unsqueeze(2).to_broadcast([P, EXPERTS, MORE])
            start_j = START.unsqueeze(2).to_broadcast([P, EXPERTS, MORE])
            pass_of = c_("pass_of").rearrange("p (e c) -> p e c", e=EXPERTS)

            def by_pass(v):
                return v.rearrange("p (e c) -> p e c", e=EXPERTS)

            shape = [P, TASKS, NJ]

            def list_passes():
                step.mark(tt_op(by_pass(MF), cnt_j, pass_of, GT))
                step.mark(V_.memset(onesrow, 1.0))
                step(ts_op(by_pass(MS), cnt_j, -float(CH), None, ADD))
                step(tt_op(by_pass(MS), by_pass(MS), pass_of, MIN))
                step(tt_op(by_pass(MS), by_pass(MS), start_j, ADD))
                step(V_.tensor_tensor_scan(MC, onesrow, MF, 0.0, MUL, ADD))
                step(tt_op(MB, MC, MF, SUB))
                step(tt_op(TOH, MB.unsqueeze(1).to_broadcast(shape), iota[:, 0:TASKS].unsqueeze(2).to_broadcast(shape),
                           EQ))
                step(tt_op(TOH, TOH, MF.unsqueeze(1).to_broadcast(shape), MUL))

            def pass_fields(ks):
                for k in ks:
                    v = MS if k == 3 else c_("units_of").rearrange("p (k j) -> p k j", k=3)[:, k, :]
                    step(tt_op(TMUL, TOH, v.unsqueeze(1).to_broadcast(shape), MUL))
                    step(V_.tensor_reduce(TASK[:, k, :], TMUL, AX.X, ADD))

            def passes_to_integers():
                step(V_.tensor_copy(taski[:, 0:4 * TASKS], TASK.rearrange("p a b -> p (a b)")))
                V_.tensor_copy(taski[:, 4 * TASKS:4 * TASKS + 1], MC[:, NJ - 1:NJ]).then_inc(tasks_ready, 1)

            def activations(par):
                return tt_op(AT[0:CH, par], SL[0:CH, par], psum[0:CH, par, D_EXP:2 * D_EXP], MUL)

            def experts(e, i=0):
                if e < EXPERTS - 1:
                    split_lo(dve, U_EXP + 2 + 3 * e, i)
                dve.wait_ge(silu_done, i * 2 + (e + 1))
                activations(e % 2).then_inc(at_ready, 1)
                if e < EXPERTS - 1:
                    split_lo(dve, U_EXP + 3 + 3 * e, i)
                split_lo(dve, U_EXP + 4 + 3 * e if e < EXPERTS - 1 else UNITS - 1, i)
                dve.wait_ge(ae_hi, i * 2 + (e + 1))
                tt_op(AEL[:, e % 2], psum[:, 4 + e % 2, 0:2 * CH].rearrange("p (f n) -> p f n", f=2),
                      AEH[:, e % 2].bitcast(fp32), SUB).then_inc(ae_lo, 1)

            experts(0)
            list_passes()
            experts(1)
            pass_fields((0, 1))
            experts(2)
            pass_fields((2, 3))
            experts(3)
            passes_to_integers()
            with dve.Fori(0, (EXPERTS - 6) // 2) as i:
                experts(4, i)
                experts(5, i)
            experts(EXPERTS - 2)
            experts(EXPERTS - 1)

            dve.wait_ge(tasks_ready, 1)
            total = dve.value_load(taski[0:1, 4 * TASKS:4 * TASKS + 1], min_val=0, max_val=TASKS)
            with dve.If(total > 0):
                dve.wait_ge(y_stored, 16 * (EXPERTS - 1))
                with dve.Fori(0, total) as t:
                    dve.wait_ge(more_silu, t + 1)
                    activations(0).then_inc(more_at, 1)
                    dve.wait_ge(more_tr, t + 1)
                    V_.tensor_copy(AE, psum[:, 4, 0:2 * CH].rearrange("p (f n) -> p f n", f=2)).then_inc(more_ae, 1)
                    dve.wait_ge(unit_used, t + (UNITS + 1))
                    V_.tensor_copy(YO[0:CH, 0, :], psum[0:CH, 2:4, :].rearrange("p a b -> p (a b)")
                                   ).then_inc(more_copied, 1)
                    dve.wait_ge(more_stored, t * 16 + 16)
                dve.nop()
            dve.nop()
            for tt in range(TT):
                dve.wait_ge(y_done, tt + 1)
                tt_op(X[:, tt, :], X[:, tt, :], psum[:, 2 * tt:2 * tt + 2, :].rearrange("p a b -> p (a b)"), ADD
                      ).then_inc(final_x, 1)
                mean_squares(9 + tt, [(0, 1, D)])
                dve.wait_ge(final_x, tt + 1)
                stt(HN[:, tt, :], X[:, tt, :], rstd[:, 9 + tt, 0:1], r_("final"), MUL, MUL).then_inc(out_ready, 1)


def constants():
    c = np.zeros((P, CC.size), np.float32)
    i, j = np.arange(P)[:, None], np.arange(P)[None, :]
    c[:, CC["ident"]] = i == j
    c[:, CC["tri"]] = i <= j
    c[:, CC["ones"]] = 1
    c[:, CC["stri"]] = i < j
    c[:, CC["btri"]] = (i <= j) & (i // GLA_CHUNK == j // GLA_CHUNK)
    q = np.arange(P)[:, None]
    c[:, CC["causal"]] = np.where(np.concatenate([j <= q, np.arange(S)[None] <= q + P], 1), 0, np.float32(NEG))
    c[:, CC["iota"]] = np.arange(SLOTS)
    inv = np.float32(10000.0) ** (-(np.arange(HALF, dtype=np.float32) * np.float32(2.0) / np.float32(ROPE)))
    ang = np.arange(S, dtype=np.float32)[:, None] * inv[None, :].astype(np.float32)
    for name, f in (("cos", np.cos), ("sin", np.sin)):
        c[:, CC[name]] = f(ang).astype(np.float32).reshape(TT, P, HALF).transpose(1, 0, 2).reshape(P, -1)
    pos = np.arange(PAD) + 1
    c[:, CC["rcount"]] = np.concatenate([1.0 / np.minimum(pos, w) for w in POOL_WINDOWS])
    dist = 2 * WINDOW - 1 - np.arange(P + S)
    d = np.maximum(dist, 1).astype(np.float32)
    exact = BUCKETS // 2
    large = exact + (np.log(d / exact) / np.float32(math.log(MAX_DIST / exact)) * (BUCKETS - exact)).astype(np.int32)
    bucket = np.where(dist < exact, dist, np.minimum(large, BUCKETS - 1))
    valid = (dist >= 0) & (dist < WINDOW)
    c[0:BUCKETS, CC["bucket"]] = (bucket[None] == np.arange(BUCKETS)[:, None]) & valid[None]
    c[0:SWA_HEADS, CC["line"]] = np.where(valid, 0, np.float32(NEG))
    for h in range(FOX_HEADS):
        c[h, CC["foxk"].start + h * S:CC["foxk"].start + (h + 1) * S] = HD ** 0.5
        c[h, CC["foxq"].start + h * P:CC["foxq"].start + (h + 1) * P] = -HD ** 0.5
    e = np.arange(EXPERTS)
    gate = np.where(e == 0, U_EXP, U_EXP - 1 + 3 * e)
    down = np.where(e == EXPERTS - 1, UNITS - 1, U_EXP + 4 + 3 * e)
    c[:, CC["units_of"]] = np.repeat(np.stack([gate, gate + 1, down]), MORE, axis=1).reshape(-1)
    c[:, CC["pass_of"]] = np.tile(CH * (1 + np.arange(MORE)), EXPERTS)
    return c


def by_columns(w, width=FF_CHUNK):
    K, N = w.shape
    return w.reshape(K // P, P, N // width, width).transpose(2, 1, 0, 3).reshape(N // width, P, UNIT)


def by_rows(w):
    K, N = w.shape
    return w.reshape(K // (2 * P), 2, P, N).transpose(0, 2, 1, 3).reshape(K // (2 * P), P, UNIT)


def interleaved(gate, up, down):
    order = [gate[0], up[0]]
    for n in range(len(gate) - 1):
        order += [gate[n + 1], up[n + 1], down[n]]
    return order + [down[-1]]


def kernel(**inputs):
    import concourse.bacc as bacc
    from concourse.bass_utils import run_bass_kernel_spmd

    a = {k: np.asarray(v) for k, v in inputs.items()}
    one = {k: v[0] for k, v in a.items() if k not in ("rel_bias", "norm_f_g_2")}

    w = one["w_in"]
    swa, fox = (SWA_HEADS + 2 * SWA_KV) * HD, 3 * FOX_HEADS * HD + FOX_HEADS
    heads = [w[:, h * HD:(h + 1) * HD] for h in range(SWA_HEADS)]
    qa = [heads[4 * k + j] for j in range(4) for k in range(2)]
    ka_va = w[:, SWA_HEADS * HD:swa]
    f = w[:, swa:swa + fox]
    m = w[:, swa + fox:]
    F = FOX_HEADS * HD
    tail = np.concatenate([m[:, Q_RANK:], f[:, 3 * F:], np.zeros((D, FF_CHUNK - KV_RANK - ROPE - FOX_HEADS), np.float32)], 1)
    cols = np.concatenate([m[:, :Q_RANK], tail, f[:, 2 * F:3 * F], ka_va, *qa, f[:, :F], f[:, F:2 * F]], 1)
    units = list(by_columns(cols)) + list(by_rows(one["w_out"]))
    up = by_columns(one["w_up"])
    units += interleaved(up[:FF_CHUNKS], up[FF_CHUNKS:], by_rows(one["w_down"]))
    w = one["w_in_2"]
    widths = (GLA_KEY, GLA_KEY, GLA_VAL, GLA_VAL, GLA_RANK, POOL_G * P, D, D)
    q, k, v, r, low, pool, gg, gp = np.split(w, np.cumsum(widths)[:-1], axis=1)
    units += list(by_columns(np.concatenate([q, k, v, pool, r, gg, gp], 1)))
    branch = [one["w_gla_branch_2"], one["w_pool_branch_2"]]
    packed = [b.reshape(4, P, 2, 512).transpose(2, 1, 0, 3).reshape(2, P, UNIT) for b in branch]
    units += [packed[n][j] for j in range(2) for n in range(2)]
    units += list(by_rows(one["w_out_2"]))
    eg, eu, ed = one["w_exp_gate_2"], one["w_exp_up_2"], one["w_exp_down_2"]
    units += interleaved([by_columns(x)[0] for x in eg], [by_columns(x)[0] for x in eu], [by_rows(x)[0] for x in ed])
    units = np.stack(units)
    assert units.shape == (UNITS, P, UNIT)

    vec = np.zeros((P, VC.size), np.float32)
    for name, src in (("attn_pre", "attn_pre_norm"), ("group", "group_norm"), ("ffn_pre", "ffn_pre_norm"),
                      ("norm1", "norm1_g_2"), ("norm2", "norm2_g_2"), ("q_lat", "q_latent_norm"),
                      ("kv_lat", "kv_latent_norm"), ("pool_scale", "pool_scale_2"), ("gla", "gla_norm_g_2"),
                      ("conv", "conv_w"), ("conv_b", "conv_b")):
        vec[:, VC[name]] = one[src].reshape(-1, P).T
    rows = np.zeros((1, RC.size), np.float32)
    router_b = np.concatenate([one["b_router_group_2"], one["b_router_expert_2"].reshape(-1)])
    for name, value in (("attn_post", one["attn_post_norm"]), ("ffn_post", one["ffn_post_norm"]),
                        ("final", a["norm_f_g_2"]), ("b_alpha", one["b_alpha_2"]), ("router_b", router_b),
                        ("forget", one["forget_bias"]), ("sinks", one["swa_sinks"])):
        rows[0, RC[name]] = value
    small = np.zeros((P, SC.size), np.float32)

    def by_k(w):
        return w.reshape(-1, P, w.shape[1]).transpose(1, 0, 2).reshape(P, -1)

    small[:, SC["uq"]] = by_k(one["w_uq"])
    small[:, SC["ukv"]] = one["w_ukv"]
    small[0:GLA_RANK, SC["w_alpha"]] = one["w_alpha_up_2"]
    small[:, SC["a_low"]] = by_k(low)
    router = np.concatenate([one["w_router_group_2"], one["w_router_expert_2"].transpose(1, 0, 2).reshape(D, EXPERTS)], 1)
    small[:, SC["router"]] = by_k(router)
    small[:, SC["pool_w"]] = one["pool_w_2"].transpose(1, 0, 2).reshape(P, -1)
    small[0:BUCKETS, SC["rel"]] = a["rel_bias"]

    x = np.ascontiguousarray(a["x"][0].reshape(TT, P, D).transpose(1, 0, 2))
    nc = bacc.Bacc("TRN2", target_bir_lowering=False, num_devices=1)
    arrays = {"x_in": x, "units_in": units, "const_in": constants(), "vec_in": vec, "rows_in": rows, "small_in": small}
    args = [nc.dram_tensor(k, v.shape, mybir.dt.float32, kind="ExternalInput").ap() for k, v in arrays.items()]
    out = nc.dram_tensor("out", [TT, P, D], mybir.dt.float32, kind="ExternalOutput").ap()
    build(nc, *args, out)
    r = run_bass_kernel_spmd(nc, [arrays], core_ids=[0])
    return r.results[0]["out"].reshape(1, S, D)
```
